# Optimizing a Trainium2 kernel written in Bass

```python
import math
import jax, jax.numpy as jnp
from jax import lax
import numpy as np

D_MODEL = 1024
BATCH = 1
SEQ = 256
DEPTH = 1

HEAD_DIM = 64
SWA_HEADS = 4
SWA_KV_HEADS = 2
SWA_WINDOW = 128
SWA_BLOCK = 128
MOBA_HEADS = 4
MOBA_BLOCK = 256
MOBA_TOPK = 3
MOBA_QCHUNK = 64
DN_HEADS = 4
DN_HEAD_DIM = 128
DN_CONV = 4
DN_CHUNK = 64
D_FF = 2816
FFN_CONV = 3

NORM_EPS = 1e-6
NEG_INF = -1e30

SWA_Q = SWA_HEADS * HEAD_DIM
SWA_KV = SWA_KV_HEADS * HEAD_DIM
MOBA_W = MOBA_HEADS * HEAD_DIM
DN_W = DN_HEADS * DN_HEAD_DIM
MIX_WIDTH = SWA_Q + MOBA_W + DN_W
IN_SPLIT_SIZES = (SWA_Q, SWA_KV, SWA_KV, MOBA_W, MOBA_W, MOBA_W, 3 * DN_W, DN_W, DN_HEADS, DN_HEADS)
IN_WIDTH = SWA_Q + 2 * SWA_KV + 3 * MOBA_W + 4 * DN_W + 2 * DN_HEADS


def rms_norm(x, w):
    xf = x.astype(jnp.float32)
    y = xf * lax.rsqrt(jnp.mean(xf * xf, axis=-1, keepdims=True) + NORM_EPS)
    return (y * w.astype(jnp.float32)).astype(x.dtype)

def l2_norm(x):
    return x * lax.rsqrt(jnp.sum(x * x, axis=-1, keepdims=True) + NORM_EPS)

def alibi_slopes():
    n = SWA_HEADS + MOBA_HEADS
    s = 2.0 ** (-8.0 * jnp.arange(1, n + 1, dtype=jnp.float32) / n)
    return s[0::2], s[1::2]

def causal_depthwise_conv(x, w):
    K = w.shape[0]
    S = x.shape[1]
    xp = jnp.pad(x, ((0, 0), (K - 1, 0), (0, 0)))
    y = xp[:, 0:S] * w[0]
    for i in range(1, K):
        y = y + xp[:, i:i + S] * w[i]
    return y

def swa_sink_attention(q, k, v, sinks, slopes):
    B, S, Hq, d = q.shape
    Hkv = k.shape[2]
    G = Hq // Hkv
    nb = S // SWA_BLOCK
    qb = q.reshape(B, nb, SWA_BLOCK, Hkv, G, d)
    kb = k.reshape(B, nb, SWA_BLOCK, Hkv, d)
    vb = v.reshape(B, nb, SWA_BLOCK, Hkv, d)

    def with_prev(t):
        prev = jnp.pad(t, ((0, 0), (1, 0), (0, 0), (0, 0), (0, 0)))[:, :-1]
        return jnp.concatenate([prev, t], axis=2)

    kk, vv = with_prev(kb), with_prev(vb)
    scores = jnp.einsum('bnqhgd,bnshd->bnhgqs', qb, kk).astype(jnp.float32) * (d ** -0.5)
    rel = jnp.arange(SWA_BLOCK)[:, None] + SWA_BLOCK - jnp.arange(2 * SWA_BLOCK)[None, :]
    kpos = (jnp.arange(nb) * SWA_BLOCK - SWA_BLOCK)[:, None] + jnp.arange(2 * SWA_BLOCK)[None, :]
    valid = ((rel >= 0) & (rel < SWA_WINDOW))[None] & (kpos >= 0)[:, None, :]
    m = slopes.astype(jnp.float32).reshape(Hkv, G)[:, :, None, None]
    scores = scores - m * rel.astype(jnp.float32)
    scores = jnp.where(valid[None, :, None, None], scores, NEG_INF)
    sink = sinks.astype(jnp.float32).reshape(Hkv, G)[:, :, None, None]
    mx = jnp.maximum(scores.max(axis=-1, keepdims=True), sink)
    p = jnp.exp(scores - mx)
    denom = p.sum(axis=-1, keepdims=True) + jnp.exp(sink - mx)
    probs = (p / denom).astype(v.dtype)
    out = jnp.einsum('bnhgqs,bnshd->bnqhgd', probs, vv)
    return out.reshape(B, S, Hq, d)

def moba_attention(q, k, v, slopes):
    B, S, H, d = q.shape
    S_pad = -(-S // MOBA_BLOCK) * MOBA_BLOCK
    pad = ((0, 0), (0, S_pad - S), (0, 0), (0, 0))
    q, k, v = jnp.pad(q, pad), jnp.pad(k, pad), jnp.pad(v, pad)
    nblk = S_pad // MOBA_BLOCK
    topk = min(MOBA_TOPK, nblk)
    kb = k.reshape(B, nblk, MOBA_BLOCK, H, d).transpose(0, 3, 1, 2, 4)
    vb = v.reshape(B, nblk, MOBA_BLOCK, H, d).transpose(0, 3, 1, 2, 4)
    k_mean = kb.astype(jnp.float32).mean(axis=3)
    nq = S_pad // MOBA_QCHUNK
    q_chunks = q.reshape(B, nq, MOBA_QCHUNK, H, d).transpose(1, 0, 3, 2, 4)
    bi = jnp.arange(B)[:, None, None, None]
    hi = jnp.arange(H)[None, :, None, None]
    m = slopes.astype(jnp.float32)[None, :, None, None]
    scale = d ** -0.5
    offs = jnp.arange(MOBA_BLOCK)

    def chunk_attend(args):
        qc, c = args
        t = c * MOBA_QCHUNK + jnp.arange(MOBA_QCHUNK)
        own = (c * MOBA_QCHUNK) // MOBA_BLOCK
        gate = jnp.einsum('bhqd,bhnd->bhqn', qc.astype(jnp.float32), k_mean)
        gate = jnp.where(jnp.arange(nblk) < own, gate, NEG_INF)
        _, idx = lax.top_k(gate, topk)
        sel_ok = idx < own
        k_sel = kb[bi, hi, idx]
        v_sel = vb[bi, hi, idx]
        s_sel = jnp.einsum('bhqd,bhqrsd->bhqrs', qc, k_sel).astype(jnp.float32) * scale
        kpos_sel = idx[..., None] * MOBA_BLOCK + offs
        s_sel = s_sel - m[..., None] * (t[:, None, None] - kpos_sel).astype(jnp.float32)
        s_sel = jnp.where(sel_ok[..., None], s_sel, NEG_INF).reshape(B, H, MOBA_QCHUNK, topk * MOBA_BLOCK)
        k_own = lax.dynamic_index_in_dim(kb, own, axis=2, keepdims=False)
        v_own = lax.dynamic_index_in_dim(vb, own, axis=2, keepdims=False)
        rel_own = t[:, None] - (own * MOBA_BLOCK + offs)[None, :]
        s_own = jnp.einsum('bhqd,bhsd->bhqs', qc, k_own).astype(jnp.float32) * scale - m * rel_own.astype(jnp.float32)
        s_own = jnp.where(rel_own >= 0, s_own, NEG_INF)
        probs = jax.nn.softmax(jnp.concatenate([s_sel, s_own], axis=-1), axis=-1).astype(v.dtype)
        p_sel = probs[..., :topk * MOBA_BLOCK].reshape(B, H, MOBA_QCHUNK, topk, MOBA_BLOCK)
        p_own = probs[..., topk * MOBA_BLOCK:]
        return (jnp.einsum('bhqrs,bhqrsd->bqhd', p_sel, v_sel)
                + jnp.einsum('bhqs,bhsd->bqhd', p_own, v_own))

    out = lax.map(chunk_attend, (q_chunks, jnp.arange(nq)))
    out = out.transpose(1, 0, 2, 3, 4).reshape(B, S_pad, H, d)
    return out[:, :S]

def gated_delta_rule(q, k, v, g, beta):
    B, S, H, dk = q.shape
    dv = v.shape[-1]
    C = DN_CHUNK
    nc = S // C

    def chunks(t):
        t = t.reshape((B, nc, C, H) + t.shape[3:])
        return jnp.moveaxis(t, 3, 1)

    q = chunks(q) * (dk ** -0.5)
    k = chunks(k)
    v = chunks(v)
    g = jnp.cumsum(chunks(g), axis=-1)
    beta = chunks(beta)
    causal = jnp.tril(jnp.ones((C, C), dtype=bool))
    strict = jnp.tril(jnp.ones((C, C), dtype=bool), -1)
    gdiff = g[..., :, None] - g[..., None, :]
    decay = jnp.where(causal, jnp.exp(jnp.where(causal, gdiff, 0.0)), 0.0)
    k_beta = k * beta[..., None]
    L = jnp.where(strict, jnp.einsum('bhnid,bhnjd->bhnij', k_beta, k) * decay, 0.0)
    rhs = jnp.concatenate([v * beta[..., None], k_beta * jnp.exp(g)[..., None]], axis=-1)
    sol = lax.linalg.triangular_solve(L + jnp.eye(C, dtype=L.dtype), rhs, left_side=True,
                                      lower=True, unit_diagonal=True)
    u, w = sol[..., :dv], sol[..., dv:]
    a_intra = jnp.einsum('bhnid,bhnjd->bhnij', q, k) * decay
    q_dec = q * jnp.exp(g)[..., None]
    g_last = g[..., -1]
    k_dec = k * jnp.exp(g_last[..., None] - g)[..., None]

    def step(state, xs):
        w_c, u_c, qd_c, a_c, kd_c, gl_c = xs
        v_new = u_c - jnp.einsum('bhcd,bhde->bhce', w_c, state)
        o = jnp.einsum('bhcd,bhde->bhce', qd_c, state) + jnp.einsum('bhij,bhje->bhie', a_c, v_new)
        state = state * jnp.exp(gl_c)[..., None, None] + jnp.einsum('bhcd,bhce->bhde', kd_c, v_new)
        return state, o

    xs = (jnp.moveaxis(w, 2, 0), jnp.moveaxis(u, 2, 0), jnp.moveaxis(q_dec, 2, 0),
          jnp.moveaxis(a_intra, 2, 0), jnp.moveaxis(k_dec, 2, 0), jnp.moveaxis(g_last, 2, 0))
    state0 = jnp.zeros((B, H, dk, dv), jnp.float32)
    _, o = lax.scan(step, state0, xs)
    return o.transpose(1, 0, 3, 2, 4).reshape(B, S, H, dv)

def hybrid_token_mixer(h, w_in, swa_sinks, dn_conv_w, dn_a_log, dn_dt_bias, dn_norm, w_out,
                       slopes_swa, slopes_moba):
    B, S, _ = h.shape
    proj = h @ w_in
    split_at = np.cumsum(IN_SPLIT_SIZES)[:-1].tolist()
    qa, ka, va, qb, kb, vb, qkv_c, z_c, b_c, a_c = jnp.split(proj, split_at, axis=-1)
    o_a = swa_sink_attention(qa.reshape(B, S, SWA_HEADS, HEAD_DIM),
                             ka.reshape(B, S, SWA_KV_HEADS, HEAD_DIM),
                             va.reshape(B, S, SWA_KV_HEADS, HEAD_DIM), swa_sinks, slopes_swa)
    o_b = moba_attention(qb.reshape(B, S, MOBA_HEADS, HEAD_DIM), kb.reshape(B, S, MOBA_HEADS, HEAD_DIM),
                         vb.reshape(B, S, MOBA_HEADS, HEAD_DIM), slopes_moba)
    qkv_c = jax.nn.silu(causal_depthwise_conv(qkv_c, dn_conv_w)).astype(jnp.float32)
    qc, kc, vc = jnp.split(qkv_c, 3, axis=-1)
    qc = l2_norm(qc.reshape(B, S, DN_HEADS, DN_HEAD_DIM))
    kc = l2_norm(kc.reshape(B, S, DN_HEADS, DN_HEAD_DIM))
    vc = vc.reshape(B, S, DN_HEADS, DN_HEAD_DIM)
    beta = jax.nn.sigmoid(b_c.astype(jnp.float32))
    g = -jnp.exp(dn_a_log.astype(jnp.float32)) * jax.nn.softplus(a_c.astype(jnp.float32) + dn_dt_bias.astype(jnp.float32))
    o_c = gated_delta_rule(qc, kc, vc, g, beta)
    o_c = rms_norm(o_c, dn_norm) * jax.nn.silu(z_c.astype(jnp.float32).reshape(B, S, DN_HEADS, DN_HEAD_DIM))
    mixed = jnp.concatenate([o_a.reshape(B, S, SWA_Q), o_b.reshape(B, S, MOBA_W),
                             o_c.reshape(B, S, DN_W).astype(h.dtype)], axis=-1)
    return mixed @ w_out

def conv_glu_ffn(h, w_up, conv_w, conv_b, w_down):
    u = causal_depthwise_conv(h @ w_up, conv_w) + conv_b
    gate, up = jnp.split(u, 2, axis=-1)
    return (jax.nn.gelu(gate, approximate=True) * up) @ w_down

def first_inputs(seed: int = 0) -> dict:
    key = jax.random.key(seed)
    ks = jax.random.split(key, 16)
    f32 = jnp.float32

    def nrm(k, shape, scale):
        return jax.random.normal(k, shape, f32) * scale

    dt = jnp.exp(jax.random.uniform(ks[6], (DEPTH, DN_HEADS), f32)
                 * (math.log(0.1) - math.log(0.001)) + math.log(0.001))
    return {
        'x': nrm(ks[0], (BATCH, SEQ, D_MODEL), 1.0),
        'mix_pre_norm': 1.0 + nrm(ks[1], (DEPTH, D_MODEL), 0.05),
        'w_in': nrm(ks[2], (DEPTH, D_MODEL, IN_WIDTH), D_MODEL ** -0.5),
        'swa_sinks': nrm(ks[3], (DEPTH, SWA_HEADS), 0.5),
        'dn_conv_w': nrm(ks[4], (DEPTH, DN_CONV, 3 * DN_W), DN_CONV ** -0.5),
        'dn_a_log': jnp.log(jax.random.uniform(ks[5], (DEPTH, DN_HEADS), f32, 1.0, 16.0)),
        'dn_dt_bias': dt + jnp.log(-jnp.expm1(-dt)),
        'dn_norm': 1.0 + nrm(ks[7], (DEPTH, DN_HEAD_DIM), 0.05),
        'w_out': nrm(ks[8], (DEPTH, MIX_WIDTH, D_MODEL), MIX_WIDTH ** -0.5),
        'mix_post_norm': 1.0 + nrm(ks[9], (DEPTH, D_MODEL), 0.05),
        'ffn_pre_norm': 1.0 + nrm(ks[10], (DEPTH, D_MODEL), 0.05),
        'w_up': nrm(ks[11], (DEPTH, D_MODEL, 2 * D_FF), D_MODEL ** -0.5),
        'ffn_conv_w': nrm(ks[12], (DEPTH, FFN_CONV, 2 * D_FF), FFN_CONV ** -0.5),
        'ffn_conv_b': nrm(ks[13], (DEPTH, 2 * D_FF), 0.02),
        'w_down': nrm(ks[14], (DEPTH, D_FF, D_MODEL), D_FF ** -0.5),
        'ffn_post_norm': 1.0 + nrm(ks[15], (DEPTH, D_MODEL), 0.05),
    }

def first_block(x, mix_pre_norm, w_in, swa_sinks, dn_conv_w, dn_a_log, dn_dt_bias, dn_norm, w_out,
              mix_post_norm, ffn_pre_norm, w_up, ffn_conv_w, ffn_conv_b, w_down, ffn_post_norm):
    slopes_swa, slopes_moba = alibi_slopes()
    for l in range(DEPTH):
        h = rms_norm(x, mix_pre_norm[l])
        mix = hybrid_token_mixer(h, w_in[l], swa_sinks[l], dn_conv_w[l], dn_a_log[l], dn_dt_bias[l],
                                 dn_norm[l], w_out[l], slopes_swa, slopes_moba)
        x = x + rms_norm(mix, mix_post_norm[l])
        h = rms_norm(x, ffn_pre_norm[l])
        x = x + rms_norm(conv_glu_ffn(h, w_up[l], ffn_conv_w[l], ffn_conv_b[l], w_down[l]), ffn_post_norm[l])
    return x


N_META = 16
CHUNK = 128
PAD = CHUNK - N_META
CONF_WIDTH = D_MODEL
CONF_KERNEL = 31
SSM_INNER = 2 * D_MODEL
SSM_HEAD_DIM = 64
SSM_HEADS = SSM_INNER // SSM_HEAD_DIM
SSM_GROUPS = 4
SSM_STATE = 128
SSM_CONV = 7
XBC_WIDTH = SSM_INNER + 2 * SSM_GROUPS * SSM_STATE
N_BRANCHES = 2
N_EXPERTS = 16
CAPACITY_FACTOR = 2
EXPERT_FF = 2 * D_MODEL
OFF_CONF = 0
OFF_Z = OFF_CONF + 2 * CONF_WIDTH
OFF_XBC = OFF_Z + SSM_INNER
OFF_DT = OFF_XBC + XBC_WIDTH
OFF_GATE = OFF_DT + 2 * SSM_HEADS
IN_WIDTH_2 = OFF_GATE + N_BRANCHES * D_MODEL
EPS = 1e-6


def rms_norm_2(x, w):
    xf = x.astype(jnp.float32)
    y = xf * lax.rsqrt(jnp.mean(xf * xf, axis=-1, keepdims=True) + EPS)
    return (y * w.astype(jnp.float32)).astype(x.dtype)

def layer_norm(x, g, b):
    xf = x.astype(jnp.float32)
    mu = jnp.mean(xf, axis=-1, keepdims=True)
    var = jnp.mean(jnp.square(xf - mu), axis=-1, keepdims=True)
    y = (xf - mu) * lax.rsqrt(var + EPS)
    return (y * g.astype(jnp.float32) + b.astype(jnp.float32)).astype(x.dtype)

def depthwise_conv(x, w, b):
    y = lax.conv_general_dilated(x, w[:, None, :].astype(x.dtype), window_strides=(1,), padding='SAME',
                                 dimension_numbers=('NWC', 'WIO', 'NWC'), feature_group_count=x.shape[-1])
    return y + b.astype(x.dtype)

def pad_front(a):
    return jnp.pad(a, [(0, 0), (PAD, 0)] + [(0, 0)] * (a.ndim - 2))

def ssd_scan(x, dt, A, B, C):
    b, T, h, p = x.shape
    g, n = B.shape[2], B.shape[3]
    j = h // g
    c = T // CHUNK
    xd = (x * dt[..., None]).reshape(b, c, CHUNK, g, j, p)
    a = jnp.moveaxis((dt * A).reshape(b, c, CHUNK, g, j), 2, -1)
    a_cs = jnp.cumsum(a, axis=-1)
    Bc = B.reshape(b, c, CHUNK, g, n)
    Cc = C.reshape(b, c, CHUNK, g, n)
    seg = a_cs[..., :, None] - a_cs[..., None, :]
    mask = jnp.tril(jnp.ones((CHUNK, CHUNK), dtype=bool))
    decay = jnp.exp(jnp.where(mask, seg, -jnp.inf))
    cb = jnp.einsum('bclgn,bcsgn->bcgls', Cc, Bc)
    y_diag = jnp.einsum('bcgls,bcgjls,bcsgjp->bclgjp', cb, decay, xd)
    decay_to_end = jnp.exp(a_cs[..., -1:] - a_cs)
    states = jnp.einsum('bclgn,bcgjl,bclgjp->bcgjpn', Bc, decay_to_end, xd)
    chunk_decay = jnp.exp(a_cs[..., -1])

    def step(carry, inp):
        st, dec = inp
        return carry * dec[..., None, None] + st, carry

    init = jnp.zeros((b, g, j, p, n), dtype=states.dtype)
    _, prev = lax.scan(step, init, (jnp.moveaxis(states, 1, 0), jnp.moveaxis(chunk_decay, 1, 0)))
    prev = jnp.moveaxis(prev, 0, 1)
    y_off = jnp.einsum('bclgn,bcgjpn,bcgjl->bclgjp', Cc, prev, jnp.exp(a_cs))
    return (y_diag + y_off).reshape(b, T, h, p)

def bidir_ssd(xs, dt_raw, dt_bias, a_log, Bs, Cs, d_skip):
    f32 = jnp.float32
    xf, Bf, Cf = xs.astype(f32), Bs.astype(f32), Cs.astype(f32)
    dtr = dt_raw.astype(f32)
    dt_f = jax.nn.softplus(dtr[..., :SSM_HEADS] + dt_bias[0].astype(f32))
    dt_b = jax.nn.softplus(dtr[..., SSM_HEADS:] + dt_bias[1].astype(f32))
    A = -jnp.exp(a_log.astype(f32))
    xp, Bp, Cp = pad_front(xf), pad_front(Bf), pad_front(Cf)
    y_f = ssd_scan(xp, pad_front(dt_f), A[0], Bp, Cp)
    fl = lambda t: jnp.flip(t, axis=1)
    y_b = fl(ssd_scan(fl(xp), fl(pad_front(dt_b)), A[1], fl(Bp), fl(Cp)))
    y = (y_f + y_b)[:, PAD:] + d_skip.astype(f32)[:, None] * xf
    return y.astype(xs.dtype)

def expert_choice_ffn(xn, w_router, w_gate, w_up, w_down):
    b, T, d = xn.shape
    cap = CAPACITY_FACTOR * T // N_EXPERTS
    aff = jax.nn.softmax(jnp.einsum('btd,de->bte', xn, w_router).astype(jnp.float32), axis=-1)
    top_aff, top_idx = lax.top_k(jnp.swapaxes(aff, 1, 2), cap)
    bi = jnp.arange(b)[:, None, None]
    xg = xn[bi, top_idx]
    hg = jnp.einsum('becd,edf->becf', xg, w_gate)
    hu = jnp.einsum('becd,edf->becf', xg, w_up)
    y = jnp.einsum('becf,efd->becd', jax.nn.silu(hg) * hu, w_down)
    y = y * top_aff[..., None].astype(y.dtype)
    return jnp.zeros_like(xn).at[bi, top_idx].add(y)

def second_inputs(seed: int = 0) -> dict:
    key = jax.random.key(seed)
    ks = jax.random.split(key, 24)
    f32 = jnp.float32
    nrm = lambda k, shape, scale: jax.random.normal(k, shape, f32) * scale
    gain = lambda k, shape: 1.0 + 0.02 * jax.random.normal(k, shape, f32)
    L = DEPTH
    dt0 = jnp.exp(jax.random.uniform(ks[10], (L, 2, SSM_HEADS), f32, np.log(1e-3), np.log(1e-1)))
    dt_bias = dt0 + jnp.log(-jnp.expm1(-dt0))
    a_log = jnp.log(jax.random.uniform(ks[11], (L, 2, SSM_HEADS), f32, 1.0, 16.0))
    return {
        "x": jax.random.normal(ks[0], (BATCH, SEQ, D_MODEL), f32),
        "meta_tokens": nrm(ks[1], (N_META, D_MODEL), 1.0),
        "w_norm_mix": gain(ks[2], (L, D_MODEL)),
        "w_in": nrm(ks[3], (L, D_MODEL, IN_WIDTH_2), D_MODEL ** -0.5),
        "w_conf_dw": nrm(ks[4], (L, CONF_KERNEL, CONF_WIDTH), CONF_KERNEL ** -0.5),
        "b_conf_dw": nrm(ks[5], (L, CONF_WIDTH), 0.02),
        "conf_ln_g": gain(ks[6], (L, CONF_WIDTH)),
        "conf_ln_b": nrm(ks[7], (L, CONF_WIDTH), 0.02),
        "w_conf_out": nrm(ks[8], (L, CONF_WIDTH, D_MODEL), CONF_WIDTH ** -0.5),
        "w_ssm_conv": nrm(ks[9], (L, SSM_CONV, XBC_WIDTH), SSM_CONV ** -0.5),
        "b_ssm_conv": nrm(ks[12], (L, XBC_WIDTH), 0.02),
        "ssm_dt_bias": dt_bias,
        "ssm_a_log": a_log,
        "ssm_d": gain(ks[13], (L, SSM_HEADS)),
        "w_ssm_norm": gain(ks[14], (L, SSM_INNER)),
        "w_ssm_out": nrm(ks[15], (L, SSM_INNER, D_MODEL), SSM_INNER ** -0.5),
        "w_out": nrm(ks[16], (L, D_MODEL, D_MODEL), D_MODEL ** -0.5),
        "w_norm_ffn": gain(ks[17], (L, D_MODEL)),
        "w_router": nrm(ks[18], (L, D_MODEL, N_EXPERTS), D_MODEL ** -0.5),
        "w_exp_gate": nrm(ks[19], (L, N_EXPERTS, D_MODEL, EXPERT_FF), D_MODEL ** -0.5),
        "w_exp_up": nrm(ks[20], (L, N_EXPERTS, D_MODEL, EXPERT_FF), D_MODEL ** -0.5),
        "w_exp_down": nrm(ks[21], (L, N_EXPERTS, EXPERT_FF, D_MODEL), EXPERT_FF ** -0.5),
        "w_norm_final": gain(ks[22], (D_MODEL,)),
    }

def second_block(x, meta_tokens, w_norm_mix, w_in, w_conf_dw, b_conf_dw, conf_ln_g, conf_ln_b, w_conf_out,
              w_ssm_conv, b_ssm_conv, ssm_dt_bias, ssm_a_log, ssm_d, w_ssm_norm, w_ssm_out, w_out,
              w_norm_ffn, w_router, w_exp_gate, w_exp_up, w_exp_down, w_norm_final):
    b = x.shape[0]
    meta = jnp.broadcast_to(meta_tokens[None].astype(x.dtype), (b, N_META, D_MODEL))
    h = jnp.concatenate([meta, x], axis=1)
    Lt = h.shape[1]
    for l in range(DEPTH):
        u = rms_norm_2(h, w_norm_mix[l])
        proj = jnp.einsum('btd,dk->btk', u, w_in[l])
        conf_a = proj[..., OFF_CONF:OFF_CONF + CONF_WIDTH]
        conf_g = proj[..., OFF_CONF + CONF_WIDTH:OFF_Z]
        z = proj[..., OFF_Z:OFF_XBC]
        xbc = proj[..., OFF_XBC:OFF_DT]
        dt_raw = proj[..., OFF_DT:OFF_GATE]
        gates = jax.nn.sigmoid(proj[..., OFF_GATE:].astype(jnp.float32)).astype(h.dtype)

        c = conf_a * jax.nn.sigmoid(conf_g)
        c = depthwise_conv(c, w_conf_dw[l], b_conf_dw[l])
        c = jax.nn.silu(layer_norm(c, conf_ln_g[l], conf_ln_b[l]))
        branch_conf = jnp.einsum('btc,cd->btd', c, w_conf_out[l])

        xbc = jax.nn.silu(depthwise_conv(xbc, w_ssm_conv[l], b_ssm_conv[l]))
        xs = xbc[..., :SSM_INNER].reshape(b, Lt, SSM_HEADS, SSM_HEAD_DIM)
        Bs = xbc[..., SSM_INNER:SSM_INNER + SSM_GROUPS * SSM_STATE].reshape(b, Lt, SSM_GROUPS, SSM_STATE)
        Cs = xbc[..., SSM_INNER + SSM_GROUPS * SSM_STATE:].reshape(b, Lt, SSM_GROUPS, SSM_STATE)
        y = bidir_ssd(xs, dt_raw, ssm_dt_bias[l], ssm_a_log[l], Bs, Cs, ssm_d[l]).reshape(b, Lt, SSM_INNER)
        y = rms_norm_2(y * jax.nn.silu(z), w_ssm_norm[l])
        branch_ssm = jnp.einsum('btc,cd->btd', y, w_ssm_out[l])

        merged = gates[..., :D_MODEL] * branch_conf + gates[..., D_MODEL:] * branch_ssm
        h = h + jnp.einsum('btd,de->bte', merged, w_out[l])

        hn = rms_norm_2(h, w_norm_ffn[l])
        h = h + expert_choice_ffn(hn, w_router[l], w_exp_gate[l], w_exp_up[l], w_exp_down[l])
    return rms_norm_2(h[:, N_META:], w_norm_final)


def setup_inputs(seed=0):
    out = dict(first_inputs(seed))
    for name, value in second_inputs(seed + 1).items():
        if name != "x":
            out[name + "_2"] = value
    return out


def reference(
    x, mix_pre_norm, w_in, swa_sinks, dn_conv_w, dn_a_log, dn_dt_bias, dn_norm, w_out,
    mix_post_norm, ffn_pre_norm, w_up, ffn_conv_w, ffn_conv_b, w_down, ffn_post_norm,
    meta_tokens_2, w_norm_mix_2, w_in_2, w_conf_dw_2, b_conf_dw_2, conf_ln_g_2, conf_ln_b_2,
    w_conf_out_2, w_ssm_conv_2, b_ssm_conv_2, ssm_dt_bias_2, ssm_a_log_2, ssm_d_2, w_ssm_norm_2,
    w_ssm_out_2, w_out_2, w_norm_ffn_2, w_router_2, w_exp_gate_2, w_exp_up_2, w_exp_down_2,
    w_norm_final_2,
):
    x = first_block(
        x, mix_pre_norm, w_in, swa_sinks, dn_conv_w, dn_a_log, dn_dt_bias, dn_norm, w_out,
        mix_post_norm, ffn_pre_norm, w_up, ffn_conv_w, ffn_conv_b, w_down, ffn_post_norm,
    )
    return second_block(
        x, meta_tokens_2, w_norm_mix_2, w_in_2, w_conf_dw_2, b_conf_dw_2, conf_ln_g_2,
        conf_ln_b_2, w_conf_out_2, w_ssm_conv_2, b_ssm_conv_2, ssm_dt_bias_2, ssm_a_log_2,
        ssm_d_2, w_ssm_norm_2, w_ssm_out_2, w_out_2, w_norm_ffn_2, w_router_2, w_exp_gate_2,
        w_exp_up_2, w_exp_down_2, w_norm_final_2,
    )


_drawn_inputs = setup_inputs


def setup_inputs(seed=0):
    import zlib

    import numpy as np

    out = dict(_drawn_inputs(seed))
    spreads = {}
    factors = {'ffn_conv_b': 2.843,
     'w_norm_mix_2': 4.709,
     'b_conf_dw_2': 5.786,
     'conf_ln_g_2': 8.0,
     'conf_ln_b_2': 8.0,
     'b_ssm_conv_2': 5.005,
     'ssm_d_2': 8.0,
     'w_ssm_norm_2': 6.922,
     'w_norm_ffn_2': 6.382,
     'w_norm_final_2': 2.951}
    for name, (base, spread) in spreads.items():
        noise = np.random.default_rng([zlib.crc32(name.encode()), seed]).standard_normal(out[name].shape)
        drawn = base * np.exp(spread * noise) if base else spread * noise
        out[name] = __import__('jax').numpy.asarray(drawn.astype(out[name].dtype))
    for name, factor in factors.items():
        out[name] = (out[name] * factor).astype(out[name].dtype)
    return out
```

```python
from contextlib import ExitStack

import concourse.bass as bass
from concourse import mybir

F32 = mybir.dt.float32
ALU = mybir.AluOpType
ACT = mybir.ActivationFunctionType
AX = mybir.AxisListType.X

P = 128
S = 256
META = 16
T = META + S
D = 1024
DC = D // P
PW = 256
EPS = 1e-6
NEG = -1e30
HD = 64
NH = 8
DNH = 4
DFF = 2816
FB = DFF // P
SH = 32
SG = 4
E = 16
CAP = 2 * T // E
EFF = 2048
EB = EFF // P
RING = 6
TOK = [(0, META), (META, P), (META + P, P)]
GELU_A = 0.044715
GELU_B = 2.0 * 0.7978845608028654

PAR_ROWS = [("mix_pre", 8), ("mix_post", 8), ("ffn_pre", 8), ("ffn_post", 8), ("dn_norm", 1),
            ("dn_conv", 48), ("ffn_conv", 132), ("ffn_b", 44), ("mix2", 8), ("conf_w", 248),
            ("conf_b", 8), ("ln_g", 8), ("ln_b", 8), ("ssm_w", 168), ("ssm_b", 24),
            ("ssm_norm", 16), ("ffn2", 8)]
PAR = {}
_n = 0
for _name, _rows in PAR_ROWS:
    PAR[_name] = _n
    _n += _rows
PAR_N = _n
PAR_T = (PAR_N + P - 1) // P

CONTINUES = {"E_done": ("PT_done", 14), "M_ready": ("BT_ready", 14), "acc_done": ("LT_ready", 2),
             "affT_copied": ("XT_ready", 14), "aff_ready": ("X_ready", 12), "aff_turned": ("PX_done", 12),
             "bs_ready": ("Y_copied", 14), "bt_copied": ("dec_read", 2), "bt_done": ("Y_done", 14),
             "cb_done": ("bB_done", 2), "cb_ready": ("aT_ready", 2), "centred": ("ba_copied", 1),
             "cg_ready": ("ex12_ready", 2), "conf_conv": ("ba_ready", 1), "conf_ready": ("bd_ready", 2),
             "conv6": ("conv_ready", 1), "csig_ready": ("expG_read", 1), "dt_copied": ("gate_w", 1),
             "dt_done": ("ba_done", 1), "dt_exp": ("exps_ready", 2), "dt_ln": ("ez_ready", 1),
             "dt_neg": ("heads_copied", 2), "dt_w": ("kb_ready", 2), "dta_ready": ("mixed_ready", 1),
             "esig_ready": ("gate_exp", 1), "ex_done": ("gate_ln", 1), "ex_out": ("gexp_read", 1),
             "g6_ready": ("par_copied", 2), "gathered": ("dec_done", 2), "group_left": ("probs_ready", 2),
             "gsig_ready": ("o_copied", 2), "h2_ready": ("q_ready", 1), "h_ready": ("qk_ready", 1),
             "hacc_copied": ("res_ready", 1), "hacc_turned": ("expG_done", 1), "hn_ready": ("rhs_ready", 1),
             "hn_tok_copied": ("probsT_copied", 6), "hn_turned": ("gsum_done", 1), "lg_copied": ("scores_read", 2),
             "lg_done": ("heads_done", 2), "lg_exp": ("raw1_ready", 1), "lg_shifted": ("shifted", 2),
             "ln_ready": ("silu_ready", 2), "mean_done": ("kk_done", 2), "mean_read": ("vn1_ready", 1),
             "merged_ready": ("vtok_ready", 2), "mo_ready": ("rn_ln", 4), "oh_ready": ("x_copied", 5),
             "oh_turned": ("kq_done", 2), "pads_ready": ("ffn_pad", 1), "pos_turned": ("o_done", 2),
             "rfin_ready": ("rn_ready", 1), "row_exp": ("ro_ln", 2), "scattered": ("par_turned", 2),
             "sig6": ("ro_ready", 1), "st_done": ("probsT_done", 6), "sums_done": ("rn_sum", 4),
             "sums_read": ("st1_copied", 1), "xbc_ready": ("tok_copied", 4), "xg_ready": ("u_copied", 2),
             "xt_done": ("ro_sum", 2), "y_done": ("scores_done", 2), "yt_done": ("st1_done", 1),
             "zsig_ready": ("wT_copied", 1)}


def two_blocks(nc, a, out):
    with ExitStack() as ctx:
        events = {}

        after = {name: count for name, (_, count) in CONTINUES.items()}

        def ev(name):
            name = CONTINUES[name][0] if name in CONTINUES else name
            if name not in events:
                events[name] = ctx.enter_context(nc.semaphore(name))
            return events[name]

        arena = ctx.enter_context(nc.sbuf_tensor("arena", [P, 53000], F32))
        top = [0]

        def cut(*shape):
            n = 1
            for s in shape:
                n *= s
            ap = arena[:, top[0]:top[0] + n]
            top[0] += n
            assert top[0] <= 53000, (top[0], shape)
            if len(shape) == 2:
                ap = ap.rearrange("p (a b) -> p a b", a=shape[0])
            elif len(shape) == 3:
                ap = ap.rearrange("p (a b c) -> p a b c", a=shape[0], b=shape[1])
            return ap

        psum = ctx.enter_context(nc.psum_tensor("psum", [P, 8, 512], F32))
        G = [psum[:, 4 + b, :] for b in range(4)]

        hT = cut(DC, T)
        ident, ones = cut(P), cut(P)
        m_le, m_gt, m_lt, m_ge = cut(P), cut(P), cut(P), cut(P)
        par = cut(PAR_T * P)
        esmall = cut(64)
        w_dt = cut(DC, 2 * SH)
        w_r = cut(DC, E)
        row_dt, row_al = cut(2 * SH), cut(2 * SH)
        d_col = cut(2 * SH // 4)
        slots_iota = cut(CAP)
        dense = [cut(11 * PW) for _ in range(2)]
        base_all = top[0]

        def pcol(name, i=0):
            return par[:, PAR[name] + i:PAR[name] + i + 1]

        def pdyn(name, i):
            return par[:, bass.ds(i + PAR[name], 1)]

        uT = cut(DC, T)
        sq = cut(DC, T)
        rs = cut(512)
        mark1 = top[0]
        raw1 = cut(26, 260)
        mixed = cut(8, S)
        w_ba = cut(DC, 8)
        ba = cut(2, 8)
        gates1 = cut(2, 24)
        bc_row = cut(64)
        qkv = cut(12, S)
        mark_at = top[0]
        bias = cut(NH, S)
        relf = cut(S)
        slopes_t = cut(8)
        q_arr = cut(2, S)
        vtok = cut(2, 3, P)
        sc = cut(NH * S)
        pT = cut(2 * NH * P)
        mx, den, esink = cut(8), cut(8), cut(4)
        attn_end = top[0]
        top[0] = mark_at
        ex12 = cut(12 * S)
        attn_end = max(attn_end, top[0], mark_at + 17 * 4 * P)
        top[0] = attn_end
        lvl = cut(7, P)
        rn = cut(8, S)
        ktok, vtok2 = cut(2, 4, P), cut(2, 4, P)
        mg = [cut(4, P) for _ in range(2)]
        dec = [cut(4, P) for _ in range(2)]
        bB = [cut(4, P) for _ in range(2)]
        LT = [cut(4, P) for _ in range(2)]
        aT = [cut(4, P) for _ in range(2)]
        expG = cut(4, P)
        top[0] = mark_at
        X = [cut(4, P) for _ in range(2)]
        XT = [cut(4, P) for _ in range(2)]
        BT = [cut(4, P) for _ in range(2)]
        Y = [cut(4, P) for _ in range(2)]
        vb = [cut(4, P) for _ in range(2)]
        kbg, kdec, qdec, st1, wT, vn1 = [cut(4, P) for _ in range(6)]
        vn0 = cut(4, P)
        assert top[0] <= attn_end
        oT = rn[:, 0:4, :]
        sz = rn[:, 4:8, :]
        ez = ktok
        mT = qkv[:, 0:8, :]

        top[0] = mark1
        raw_ff = cut(2 * FB, S + 2)
        hid = cut(FB, S)
        fT = cut(DC, S)

        xtok = sc.rearrange("p (a b) -> p a b", a=2)
        meta_tok = pT[:, 0:D]
        par_rows = pT[:, D:D + PAR_T * P].rearrange("p (a b) -> p a b", a=PAR_T)
        sq_dn = sq.rearrange("p a b -> p (a b)")[:, 0:8 * S]
        ro = qkv[:, 8:12, :].rearrange("p a b -> p (a b)")
        eps_t = esmall[:, 0:1]
        gx, ux, fg, fe = [cut(2, S) for _ in range(4)]

        top[0] = mark1
        raw_cf = cut(16, T)
        yT = raw_cf
        cpad = cut(DC, T + 30)
        bcf = cpad.rearrange("p a b -> p (a b)")[:, 0:DC * T].rearrange("p (a b) -> p a b", a=DC)
        cc = cut(DC, T)
        work2 = cc.rearrange("p a b -> p (a b)")[:, 0:2 * 8 * P].rearrange("p (x h l) -> p x h l", x=2, h=8)
        gts = cut(16, T)
        xraw = cut(24, T + 6)
        xrawf = xraw.rearrange("p a b -> p (a b)")
        sqy = xrawf[:, 0:16 * T].rearrange("p (a b) -> p a b", a=16)
        bs = xrawf[:, 16 * T:24 * T].rearrange("p (a b) -> p a b", a=DC)
        upper = top[0]
        zT = cut(16, T)
        g7 = cut(7, T)
        g6 = g7[:, 1:7, :]
        b_tok = cut(3, P)
        xdf, xdb = cut(3, 512), cut(3, 512)
        xef, xeb = cut(2, 512), cut(2, 512)
        st = cut(4, 512)
        cbf, cbb = cut(272), cut(272)
        ytok = cut(3, 512)
        dts, dta, dtw, dtx = [cut(3, 2 * SH) for _ in range(4)]
        dte = cut(3, 2 * SH)
        sums = cut(7 * 2 * SH)
        mo = cc
        small2 = [work2[0:META, x, 0, :].rearrange("p (h l) -> p h l", h=8) for x in range(2)]
        six = sq.rearrange("p a b -> p (a b)")[:, 0:6 * T].rearrange("p (a b) -> p a b", a=6)

        top[0] = upper
        ring = [cut(4096) for _ in range(3)]
        es, up_row = cut(2, 512), cut(2, 512)
        top[0] = mark1
        ring += [cut(4096) for _ in range(3)]
        hn_tok = cut(3, D)
        hacc = cut(2, D)
        h_row = cut(4, 512)
        assert top[0] <= upper
        top[0] = mark1 - 512 - DC * T
        lg, pos_t, aff = cut(3, E), cut(3, E + 1), cut(3, E + 1)
        lmx = cut(3)
        oh = cut(3, CAP)
        ohs = cut(2, CAP)
        otT = cut(S)
        m8 = cut(8)
        ss = cut(4)
        assert top[0] <= mark1 - 512
        top[0] = base_all - 2 * 11 * PW
        ysb = cut(D)
        hx = cut(EB, CAP)
        xg = cut(DC, CAP)
        affT, left, pos = cut(T), cut(T), cut(T)
        wfin = cut(D)
        assert top[0] <= base_all
        ring_loaded = [ev(f"ring{k}_loaded") for k in range(RING)]
        ring_done = [ev(f"ring{k}_done") for k in range(RING)]
        r_up = [r.rearrange("p (c n) -> p c n", c=DC) for r in ring]
        r_dn = [r.rearrange("p (c n) -> p c n", c=4) for r in ring]
        GROUP_PANEL = 79

        def par_loads():
            src = {"mix_pre": a["mix_pre_norm"], "mix_post": a["mix_post_norm"], "ffn_pre": a["ffn_pre_norm"],
                   "ffn_post": a["ffn_post_norm"], "dn_norm": a["dn_norm"], "dn_conv": a["dn_conv_w"],
                   "ffn_conv": a["ffn_conv_w"], "ffn_b": a["ffn_conv_b"], "mix2": a["w_norm_mix_2"],
                   "conf_w": a["w_conf_dw_2"], "conf_b": a["b_conf_dw_2"], "ln_g": a["conf_ln_g_2"],
                   "ln_b": a["conf_ln_b_2"], "ssm_w": a["w_ssm_conv_2"], "ssm_b": a["b_ssm_conv_2"],
                   "ssm_norm": a["w_ssm_norm_2"], "ffn2": a["w_norm_ffn_2"]}
            for name, rows in PAR_ROWS:
                v = src[name]
                flat = v[0].rearrange("k (c p) -> (k c) p", p=P) if len(v.shape) == 3 else v.rearrange("a (c p) -> (a c) p", p=P)
                done = 0
                while done < rows:
                    r = PAR[name] + done
                    m = min(rows - done, P - r % P)
                    yield par_rows[r % P:r % P + m, r // P, :], flat[done:done + m, :]
                    done += m

        PAR_LOADS = len(list(par_loads()))

        def bcast(ap, n, axis=2):
            return ap.unsqueeze(axis).to_broadcast(
                [ap.shape[0], ap.shape[1], n] if axis == 2 else [ap.shape[0], n, ap.shape[1]])

        slot_loaded = [ev(f"slot{k}_loaded") for k in range(2)]
        panel_done = [ev(f"panel_done{k}") for k in range(2)]
        copied = [ev(f"pair{k}_copied") for k in range(2)]
        slot8 = [s[:, 0:DC * PW].rearrange("p (c n) -> p c n", c=DC) for s in dense]
        slot11 = [s.rearrange("p (c n) -> p c n", c=11) for s in dense]
        pair = [psum[:, 2 * k:2 * k + 2, :] for k in range(2)]

        w_in_v = a["w_in"][0].rearrange("(c p) n -> p c n", p=P)

        block = ctx.enter_context(nc.Block())

        @block.sync
        def _(sp):
            n = [0]

            def panel(src, view=slot8):
                k = n[0] % 2
                if n[0] >= 2:
                    sp.wait_ge(panel_done[k], n[0] // 2)
                sp.dma_start(view[k], src).then_inc(slot_loaded[k], 16)
                n[0] += 1

            def panels(w, count, view=slot8):
                if n[0] < 2:
                    panel(w[:, :, 0:PW])
                    panel(w[:, :, PW:2 * PW])
                    first = 1
                else:
                    first = 0
                base = n[0]
                with sp.Fori(first, count // 2) as i:
                    for j in range(2):
                        k = (base + j) % 2
                        sp.wait_ge(panel_done[k], i + ((base + j) // 2 - first))
                        sp.dma_start(view[k], w[:, :, bass.ds(i * (2 * PW) + j * PW, PW)]).then_inc(slot_loaded[k], 16)
                n[0] += 2 * (count // 2 - first)
                if count % 2:
                    panel(w[:, :, (count - 1) * PW:count * PW])

            panels(w_in_v, 13)
            w = a["w_out"][0].rearrange("(c p) n -> p c n", p=P)
            panels(w, 4)
            w = a["w_up"][0].rearrange("(c p) n -> p c n", p=P)
            base = n[0]
            with sp.Fori(0, 11) as i:
                for j in range(2):
                    k = (base + j) % 2
                    sp.wait_ge(panel_done[k], i + (base + j) // 2)
                    sp.dma_start(slot8[k], w[:, :, bass.ds(i * PW + j * DFF, PW)]).then_inc(slot_loaded[k], 16)
            n[0] += 22
            w = a["w_down"][0].rearrange("(h c p) n -> h p c n", p=P, h=2)
            base = n[0]
            with sp.Fori(0, 4) as i:
                for j in range(2):
                    k = (base + j) % 2
                    sp.wait_ge(panel_done[k], i + (base + j) // 2)
                    sp.dma_start(slot11[k], w[j][:, :, bass.ds(i * PW, PW)]).then_inc(slot_loaded[k], 16)
            n[0] += 8
            w2 = a["w_in_2"][0].rearrange("(c p) n -> p c n", p=P)
            panels(w2[:, :, 0:2048], 8)
            panels(w2[:, :, 4096:7168], 12)
            panels(w2[:, :, 2048:4096], 8)
            panels(a["w_conf_out_2"][0].rearrange("(c p) n -> p c n", p=P), 4)
            base = n[0]
            assert base == GROUP_PANEL
            with sp.Fori(0, SG) as i:
                for j in range(2):
                    k = (base + j) % 2
                    sp.wait_ge(panel_done[k], i + (base + j) // 2)
                    sp.dma_start(slot8[k], w2[:, :, bass.ds(i * (2 * PW) + (7232 + j * PW), PW)]).then_inc(slot_loaded[k], 16)
            n[0] += 2 * SG
            gate_v = a["w_exp_gate_2"][0].rearrange("e (c p) n -> e p c n", p=P)
            up_v = a["w_exp_up_2"][0].rearrange("e (c p) n -> e p c n", p=P)
            down_v = a["w_exp_down_2"][0].rearrange("e (c p) n -> e p c n", p=P)

            def expert_panel(e, q):
                k = q % RING
                if q < 8:
                    src = (up_v if q % 2 else gate_v)[e][:, :, (q // 2) * 512:(q // 2 + 1) * 512]
                    sp.dma_start(r_up[k], src).then_inc(ring_loaded[k], 16)
                else:
                    src = down_v[e][:, 4 * (q - 8):4 * (q - 7), :]
                    sp.dma_start(r_dn[k], src).then_inc(ring_loaded[k], 16)

            w = a["w_ssm_out_2"][0].rearrange("(h c p) n -> h p c n", p=P, h=2)
            for g in range(4):
                for h in range(2):
                    panel(w[h][:, :, g * PW:(g + 1) * PW])
                if g < 3:
                    if g == 0:
                        sp.wait_ge(ev("yn_ready"), 2)
                    expert_panel(0, g)
            w = a["w_out_2"][0].rearrange("(c p) n -> p c n", p=P)
            for g in range(4):
                panel(w[:, :, g * PW:(g + 1) * PW])
            sp.wait_ge(ev("h2_ready"), after["h2_ready"] + 1)
            for q in range(3, 12):
                if q >= RING:
                    sp.wait_ge(ring_done[q % RING], 1)
                expert_panel(0, q)
            with sp.Fori(1, E) as e:
                for q in range(12):
                    k = q % RING
                    sp.wait_ge(ring_done[k], e * 2 + q // RING)
                    if q < 8:
                        src = (up_v if q % 2 else gate_v)[bass.ds(e, 1), :, :, (q // 2) * 512:(q // 2 + 1) * 512]
                        sp.dma_start(r_up[k], src.rearrange("e p c n -> (e p) c n")).then_inc(ring_loaded[k], 16)
                    else:
                        src = down_v[bass.ds(e, 1), :, 4 * (q - 8):4 * (q - 7), :]
                        sp.dma_start(r_dn[k], src.rearrange("e p c n -> (e p) c n")).then_inc(ring_loaded[k], 16)
            sp.wait_ge(ev("out_ready"), 1)
            sp.dma_start(out[0].rearrange("(b p) n -> p b n", p=P), hacc).then_inc(ev("stored"), 16)
            sp.wait_ge(ev("stored"), 16)

        @block.gpsimd
        def _(pool):
            g = nc.gpsimd
            g.memset(ident, 0.0)
            g.memset(ones, 1.0)
            g.memset(lvl, 0.0)
            g.drain()
            g.affine_select(ident, ident, pattern=[[-1, P]], compare_op=ALU.not_equal, fill=1.0,
                            base=0, channel_multiplier=1).then_inc(ev("ident_ready"), 1)
            g.affine_select(m_le, ones, pattern=[[1, P]], compare_op=ALU.is_ge, fill=0.0, base=0, channel_multiplier=-1)
            g.affine_select(m_gt, ones, pattern=[[-1, P]], compare_op=ALU.is_gt, fill=0.0, base=0, channel_multiplier=1)
            g.affine_select(m_lt, ones, pattern=[[1, P]], compare_op=ALU.is_gt, fill=0.0, base=0, channel_multiplier=-1)
            g.affine_select(m_ge, ones, pattern=[[-1, P]], compare_op=ALU.is_ge, fill=0.0, base=0,
                            channel_multiplier=1).then_inc(ev("masks_ready"), 1)
            g.iota(relf, pattern=[[-1, S]], base=P, channel_multiplier=1, allow_small_or_imprecise_dtypes=True)
            g.memset(raw1[:, :, 0:3], 0.0).then_inc(ev("raw1_pad"), 1)
            g.drain()
            expo = [1, 3, 5, 7, 2, 6, 4, 8]
            for h in range(NH):
                g.tensor_scalar(bias[:, h, :], relf, -(2.0 ** -expo[h]), None, ALU.mult)
            g.drain()
            g.affine_select(bias, bias, pattern=[[0, NH], [-1, S]], compare_op=ALU.is_ge, fill=NEG,
                            base=P, channel_multiplier=1)
            g.drain()
            g.affine_select(bias[:, 0:4, :], bias[:, 0:4, :], pattern=[[0, 4], [1, S]], compare_op=ALU.is_ge,
                            fill=NEG, base=-1, channel_multiplier=-1).then_inc(ev("bias_ready"), 1)
            for lv in range(7):
                s = 1 << lv
                up = lvl[:, lv, :].rearrange("p (b h r) -> p b h r", h=2, r=s)[:, :, 1, :]
                src = ones[:, 0:P // 2].rearrange("p (b r) -> p b r", r=s)
                g.affine_select(up, src, pattern=[[-2 * s, P // (2 * s)], [0, s]], compare_op=ALU.is_ge, fill=0.0,
                                base=0, channel_multiplier=1)
            g.drain()
            for lv in range(7):
                s = 1 << lv
                up = lvl[:, lv, :].rearrange("p (b h r) -> p b h r", h=2, r=s)[:, :, 1, :]
                last = g.affine_select(up, up, pattern=[[2 * s, P // (2 * s)], [0, s]], compare_op=ALU.is_gt, fill=0.0,
                                       base=s, channel_multiplier=-1)
            last.then_inc(ev("levels_ready"), 1)
            g.iota(slots_iota, pattern=[[1, CAP]], base=1, channel_multiplier=0,
                   allow_small_or_imprecise_dtypes=True).then_inc(ev("iota_ready"), 1)
            pool.wait_ge(ev("res_ready"), 1)
            g.memset(raw_ff[:, :, 0:2], 0.0).then_inc(ev("ffn_pad"), 1)
            pool.wait_ge(ev("h1_ready"), 1)
            for t in (cpad[:, :, 0:15], cpad[:, :, 15 + T:], xraw[:, :, 0:3], xraw[:, :, 3 + T:]):
                g.memset(t, 0.0).then_inc(ev("pads_ready"), 1)

        @block.tensor
        def _(pe):
            mm = nc.tensor.matmul
            n = [0]
            release = [None] * 4

            def use(b, name, val=1):
                if release[b]:
                    pe.wait_ge(ev(release[b][0]), release[b][1])
                release[b] = (name, val + after.get(name, 0))
                return G[b]

            def dense_panels(count, rhs, width):
                base = n[0]

                def one(k, m, i=None):
                    pe.wait_ge(slot_loaded[k], 16 * (m + 1) if i is None else i * 16 + 16 * (m + 1))
                    if i is not None or m:
                        pe.wait_ge(copied[k], m if i is None else i + m)
                    for b in range(2):
                        for c in range(DC):
                            ins = mm(pair[k][:, b, 0:width], slot8[k][:, c, b * P:(b + 1) * P], rhs(c),
                                     start=c == 0, stop=c == DC - 1)
                    ins.then_inc(panel_done[k], 1)

                first = 0
                if base < 2:
                    one(0, 0)
                    one(1, 0)
                    first = 1
                if count // 2 > first:
                    with pe.Fori(first, count // 2) as i:
                        for j in range(2):
                            one((base + j) % 2, (base + j) // 2, i)
                n[0] += 2 * (count // 2)
                if count % 2:
                    one(n[0] % 2, n[0] // 2)
                    n[0] += 1

            def sum_parts(bank, src, chunks, width):
                for c in range(chunks):
                    ins = mm(bank[:, 0:width], ones, src[:, c, 0:width], start=c == 0, stop=c == chunks - 1)
                return ins

            pe.wait_ge(ev("ident_ready"), 1)
            pe.wait_ge(ev("par_loaded"), 16 * PAR_LOADS)
            for q in range(2):
                bank = use(q, "par_copied", q + 1)
                for t in range(4 * q, min(4 * q + 4, PAR_T)):
                    rows = min(P, PAR_N - t * P)
                    ins = nc.tensor.transpose(bank[:, (t % 4) * P:(t % 4) * P + rows], par_rows[0:rows, t, :],
                                              ident[0:rows, 0:rows])
                ins.then_inc(ev("par_turned"), 1)
            pe.wait_ge(ev("x_loaded"), 48)
            for tb in range(2):
                for c4 in range(2):
                    bank = use(2 + c4, "x_copied", 2 * tb + c4 + 1)
                    for c in range(4):
                        ins = nc.tensor.transpose(bank[:, c * P:(c + 1) * P],
                                                  xtok[:, tb, (4 * c4 + c) * P:(4 * c4 + c + 1) * P], ident)
                    ins.then_inc(ev("x_turned"), 1)
            bank = use(2, "x_copied", 5)
            for c in range(DC):
                ins = nc.tensor.transpose(bank[:, c * META:(c + 1) * META], meta_tok[0:META, c * P:(c + 1) * P],
                                          ident[0:META, 0:META])
            ins.then_inc(ev("x_turned"), 1)
            pe.wait_ge(ev("sq_ready"), 1)
            sum_parts(use(0, "rs_ready", 1), sq, DC, S).then_inc(ev("sum_ready"), 1)
            pe.wait_ge(ev("u_ready"), 1)
            pe.wait_ge(ev("ba_loaded"), 16)
            bank = use(1, "ba_copied", 1)
            for tb in range(2):
                for c in range(DC):
                    ins = mm(bank[:, 8 * tb:8 * tb + 8], uT[:, c, tb * P:(tb + 1) * P], w_ba[:, c, :],
                             start=c == 0, stop=c == DC - 1)
            ins.then_inc(ev("ba_done"), 1)
            dense_panels(7, lambda c: uT[:, c, 0:S], S)

            pe.wait_ge(ev("raw1_ready"), 1)
            for tb in range(2):
                bank = use(tb, "vtok_ready", tb + 1)
                for j, blk in enumerate((3, 8, 9)):
                    ins = nc.tensor.transpose(bank[:, j * P:(j + 1) * P], raw1[:, blk, 3 + tb * P:3 + (tb + 1) * P], ident)
                ins.then_inc(ev("v_turned"), 1)
            for qb in range(2):
                w = P * (qb + 1)
                q0 = 3 + qb * P
                pe.wait_ge(ev("q_ready"), 1)
                for b in range(4):
                    bank = use(b, "scores_read", qb + 1)
                    for j in range(2):
                        if b < 2:
                            lo = HD * b
                            q = q_arr[lo:lo + HD, j, qb * P:(qb + 1) * P]
                            kk = raw1[lo:lo + HD, 2, 3:3 + w]
                        else:
                            lo = HD * (b - 2)
                            q = raw1[lo:lo + HD, 4 + j, q0:q0 + P]
                            kk = raw1[lo:lo + HD, 6 + j, 3:3 + w]
                        ins = mm(bank[:, j * S:j * S + w], q, kk, start=True, stop=True)
                ins.then_inc(ev("scores_done"), 1)
                dense_panels(2 + qb, lambda c: uT[:, c, 0:S], S)
                pe.wait_ge(ev("probs_ready"), qb + 1)
                nt = NH * (qb + 1)
                for g4 in range(nt // 4):
                    bank = use(g4 % 4, "probsT_copied", (2 if qb else 0) + g4 + 1)
                    for j in range(4):
                        idx = g4 * 4 + j
                        kb, h = idx // NH, idx % NH
                        ins = nc.tensor.transpose(bank[:, j * P:(j + 1) * P],
                                                  sc[:, h * w + kb * P:h * w + kb * P + P], ident)
                    ins.then_inc(ev("probsT_done"), 1)
                pe.wait_ge(ev("probsT_copied"), 2 if qb == 0 else 6)
                bank = use(0, "heads_copied", qb + 1)
                for h in range(NH):
                    if h < 4:
                        slot = h
                        v = lambda kb: vtok[:, kb, 0, HD * (h // 2):HD * (h // 2) + HD]
                    else:
                        m = h - 4
                        slot = 4 + (m % 2) * 2 + m // 2
                        v = lambda kb: vtok[:, kb, 1 + m // 2, HD * (m % 2):HD * (m % 2) + HD]
                    lo = HD * (h % 2)
                    for kb in range(qb + 1):
                        ins = mm(bank[lo:lo + HD, (h // 2) * P:(h // 2 + 1) * P], v(kb),
                                 pT[:, (kb * NH + slot) * P:(kb * NH + slot + 1) * P],
                                 start=kb == 0, stop=kb == qb, skip_group_check=True)
                ins.then_inc(ev("heads_done"), 1)

            dense_panels(1, lambda c: uT[:, c, 0:S], S)
            pe.wait_ge(ev("sq_ready"), 2)
            for b in range(4):
                bank = use(b, "rn_ln", b + 1)
                mm(bank[:, :], ones, sq_dn[:, b * 512:(b + 1) * 512], start=True, stop=True).then_inc(ev("rn_sum"), 1)
            pe.wait_ge(ev("mg_ready"), 1)
            pe.wait_ge(ev("masks_ready"), 1)
            bank = use(0, "gexp_read", 1)
            mm(bank[:, 0:4], m_le, gates1[:, 1, 8:12], start=True, stop=True)
            mm(bank[:, 4:8], m_gt, gates1[:, 0, 8:12], start=True, stop=True).then_inc(ev("gsum_done"), 1)
            for ck in range(2):
                mm(use(1 + ck, "dec_read", ck + 1), m_gt, mg[ck], start=True, stop=True).then_inc(ev("dec_done"), 1)
            mm(use(3, "expG_read", 1), ones, mg[1], start=True, stop=True).then_inc(ev("expG_done"), 1)
            for ck in range(2):
                pe.wait_ge(ev("bd_ready"), ck + 1)
                mm(use(ck, "kb_ready", ck + 1), ones, bB[ck], start=True, stop=True).then_inc(ev("bB_done"), 1)
            pe.wait_ge(ev("qk_ready"), 1)
            for what in range(2):
                if what == 1:
                    pe.wait_ge(ev("silu_ready"), 2)
                for ck in range(2):
                    bank = use(2 + ck, "tok_copied", 2 * what + ck + 1)
                    for h in range(4):
                        ins = nc.tensor.transpose(bank[:, h * P:(h + 1) * P],
                                                  qkv[:, 4 + 4 * what + h, ck * P:(ck + 1) * P], ident)
                    ins.then_inc(ev("tok_turned"), 1)
            for ck in range(2):
                pe.wait_ge(ev("kb_ready"), ck + 1)
                bank = use(0, "LT_ready", ck + 1)
                for h in range(4):
                    ins = mm(bank[:, h * P:(h + 1) * P], qkv[:, 4 + h, ck * P:(ck + 1) * P], bB[ck][:, h, :],
                             start=True, stop=True)
                ins.then_inc(ev("kk_done"), 1)
                bank = use(1, "aT_ready", ck + 1)
                for h in range(4):
                    ins = mm(bank[:, h * P:(h + 1) * P], qkv[:, 4 + h, ck * P:(ck + 1) * P],
                             qkv[:, h, ck * P:(ck + 1) * P], start=True, stop=True)
                ins.then_inc(ev("kq_done"), 1)
            for lv in range(7):
                for ck in range(2):
                    pe.wait_ge(ev("BT_ready"), 2 * lv + ck + 1)
                    bank = use(2 * ck, "Y_copied", 2 * lv + ck + 1)
                    for h in range(4):
                        ins = mm(bank[:, h * P:(h + 1) * P], BT[ck][:, h, :], X[ck][:, h, :], start=True, stop=True)
                    ins.then_inc(ev("Y_done"), 1)
                for ck in range(2):
                    pe.wait_ge(ev("Y_copied"), 2 * lv + ck + 1)
                    bank = use(2 * ck + 1, "XT_ready", 2 * lv + ck + 1)
                    for h in range(4):
                        ins = mm(bank[:, h * P:(h + 1) * P], Y[ck][:, h, :], XT[ck][:, h, :], start=True, stop=True)
                    ins.then_inc(ev("PT_done"), 1)
                    if lv < 6:
                        bank = use(2 * ck, "X_ready", 2 * lv + ck + 1)
                        for h in range(4):
                            ins = mm(bank[:, h * P:(h + 1) * P], XT[ck][:, h, :], Y[ck][:, h, :], start=True, stop=True)
                        ins.then_inc(ev("PX_done"), 1)
            pe.wait_ge(ev("XT_ready"), 14)
            pe.wait_ge(ev("rhs_ready"), 1)
            for ck in range(2):
                bank = use(ck, "u_copied", ck + 1)
                for h in range(4):
                    ins = mm(bank[:, h * P:(h + 1) * P], XT[ck][:, h, :], vb[ck][:, h, :], start=True, stop=True)
                ins.then_inc(ev("u_done"), 1)
            bank = use(2, "wT_copied", 1)
            for h in range(4):
                ins = mm(bank[:, h * P:(h + 1) * P], kbg[:, h, :], XT[1][:, h, :], start=True, stop=True)
            ins.then_inc(ev("wT_done"), 1)
            pe.wait_ge(ev("u_copied"), 1)
            bank = use(3, "st1_copied", 1)
            for h in range(4):
                ins = mm(bank[:, h * P:(h + 1) * P], kdec[:, h, :], vn0[:, h, :], start=True, stop=True)
            ins.then_inc(ev("st1_done"), 1)
            bank = use(0, "o_copied", 1)
            for h in range(4):
                ins = mm(bank[:, h * P:(h + 1) * P], vn0[:, h, :], aT[0][:, h, :], start=True, stop=True)
            ins.then_inc(ev("o_done"), 1)
            pe.wait_ge(ev("st1_copied"), 1)
            pe.wait_ge(ev("wT_copied"), 1)
            bank = use(2, "vn1_ready", 1)
            for h in range(4):
                ins = mm(bank[:, h * P:(h + 1) * P], wT[:, h, :], st1[:, h, :], start=True, stop=True)
            ins.then_inc(ev("ws_done"), 1)
            pe.wait_ge(ev("vn1_ready"), 1)
            bank = use(1, "o_copied", 2)
            for h in range(4):
                mm(bank[:, h * P:(h + 1) * P], st1[:, h, :], qdec[:, h, :], start=True, stop=False)
                ins = mm(bank[:, h * P:(h + 1) * P], vn1[:, h, :], aT[1][:, h, :], start=False, stop=True)
            ins.then_inc(ev("o_done"), 1)
            pe.wait_ge(ev("sq_ready"), 3)
            for b in range(2):
                mm(use(2 + b, "ro_ln", b + 1), ones, sq_dn[:, b * 512:(b + 1) * 512],
                   start=True, stop=True).then_inc(ev("ro_sum"), 1)
            pe.wait_ge(ev("mixed_ready"), 1)
            dense_panels(4, lambda c: mixed[:, c, :], S)
            for norm in range(2):
                pe.wait_ge(ev("sq_ready"), 4 + norm)
                sum_parts(use(norm, "rs_ready", 2 + norm), sq, DC, S).then_inc(ev("sum_ready"), 1)
            pe.wait_ge(ev("u_ready"), 2)
            dense_panels(22, lambda c: uT[:, c, 0:S], S)
            base = n[0]
            pe.wait_ge(ev("hid_ready"), FB // 2)
            with pe.Fori(0, 4) as i:
                for j in range(2):
                    k, m = (base + j) % 2, (base + j) // 2
                    pe.wait_ge(slot_loaded[k], i * 16 + 16 * (m + 1))
                    if j == 0:
                        pe.wait_ge(copied[base % 2], i + m)
                        pe.wait_ge(copied[(base + 1) % 2], i + (base + 1) // 2)
                    for b in range(2):
                        for c in range(11):
                            ins = mm(pair[base % 2][:, b, 0:S], slot11[k][:, c, b * P:(b + 1) * P], hid[:, 11 * j + c, :],
                                     start=j == 0 and c == 0, stop=j == 1 and c == 10)
                    ins.then_inc(panel_done[k], 1)
            n[0] += 8
            pe.wait_ge(ev("sq_ready"), 6)
            sum_parts(use(2, "rs_ready", 4), sq, DC, S).then_inc(ev("sum_ready"), 1)

            pe.wait_ge(ev("sq_ready"), 7)
            sum_parts(use(0, "rs_ready", 5), sq, DC, T).then_inc(ev("sum_ready"), 1)
            pe.wait_ge(ev("u_ready"), 3)
            pe.wait_ge(ev("small_loaded"), 64)
            bank = use(1, "dt_copied", 1)
            for ck, (t0, nt) in enumerate(TOK):
                for c in range(DC):
                    ins = mm(bank[0:nt, ck * 64:(ck + 1) * 64], uT[:, c, t0:t0 + nt], w_dt[:, c, :],
                             start=c == 0, stop=c == DC - 1)
            ins.then_inc(ev("dt_done"), 1)
            dense_panels(8, lambda c: uT[:, c, :], T)
            dense_panels(12, lambda c: uT[:, c, :], T)
            dense_panels(4, lambda c: uT[:, c, :], T)
            pe.wait_ge(ev("conf_conv"), after["conf_conv"] + 1)
            sum_parts(use(0, "mean_read", 1), cc, DC, T).then_inc(ev("mean_done"), 1)
            dense_panels(2, lambda c: uT[:, c, :], T)
            pe.wait_ge(ev("sq_ready"), 8)
            sum_parts(use(1, "rs_ready", 6), sq, DC, T).then_inc(ev("sum_ready"), 1)
            dense_panels(2, lambda c: uT[:, c, :], T)
            pe.wait_ge(ev("dta_ready"), after["dta_ready"] + 1)
            bank = use(2, "sums_read", 1)
            for ck in (1, 2):
                o = 0 if ck == 1 else 192
                mm(bank[:, o:o + 32], m_le, dta[:, ck, 0:32], start=True, stop=True)
                mm(bank[:, o + 32:o + 64], m_ge, dta[:, ck, 32:64], start=True, stop=True)
                mm(bank[:, o + 64:o + 96], m_gt, dta[:, ck, 0:32], start=True, stop=True)
                mm(bank[:, o + 96:o + 128], m_lt, dta[:, ck, 32:64], start=True, stop=True)
            mm(bank[:, 128:192], ones, dta[:, 1, :], start=True, stop=True)
            n0 = META
            mm(bank[0:n0, 320:352], m_le[0:n0, 0:n0], dta[0:n0, 0, 0:32], start=True, stop=True)
            mm(bank[0:n0, 352:384], m_ge[0:n0, 0:n0], dta[0:n0, 0, 32:64], start=True, stop=True)
            mm(bank[0:n0, 384:416], m_gt[0:n0, 0:n0], dta[0:n0, 0, 0:32], start=True, stop=True)
            mm(bank[0:n0, 416:448], m_lt[0:n0, 0:n0], dta[0:n0, 0, 32:64], start=True,
               stop=True).then_inc(ev("sums_done"), 1)
            pe.wait_ge(ev("conf_ready"), after["conf_ready"] + 1)
            dense_panels(4, lambda c: cc[:, c, :], T)

            base = n[0]
            pe.wait_ge(ev("sums_read"), after["sums_read"] + 1)

            def group(i):
                def dense_half(j, b):
                    k, m = (base + j) % 2, (base + j) // 2
                    if b == 0:
                        pe.wait_ge(slot_loaded[k], i * 16 + 16 * (m + 1))
                        pe.wait_ge(copied[k], i + m)
                    for c in range(DC):
                        ins = mm(pair[k][:, b, 0:T], slot8[k][:, c, b * P:(b + 1) * P], uT[:, c, :],
                                 start=c == 0, stop=c == DC - 1)
                    if b:
                        ins.then_inc(panel_done[k], 1)

                pe.wait_ge(ev("group_left"), after["group_left"] + i + 1)
                def carry_wait():
                    mm(G[3][0:32, 0:2], ident[:, 0:32], ident[:, 0:2], start=True, stop=True)

                pe.wait_ge(ev("g6_ready"), after["g6_ready"] + i + 1)
                for ck, (t0, nt) in enumerate(TOK):
                    for b in range(4):
                        ins = nc.tensor.transpose(G[ck][0:nt, b * P:(b + 1) * P], g6[:, b, t0:t0 + nt], ident)
                    ins.then_inc(ev("xt_done"), 1)
                for ck, (t0, nt) in enumerate(TOK):
                    ins = nc.tensor.transpose(G[3][0:nt, ck * P:(ck + 1) * P], g6[:, 4, t0:t0 + nt], ident)
                ins.then_inc(ev("bt_done"), 1)
                pe.wait_ge(ev("bt_copied"), after["bt_copied"] + i + 1)
                mm(G[3][:, 0:P], g6[:, 4, META:META + P], g7[:, 0, META:META + P], start=True, stop=True)
                mm(G[3][:, P:2 * P], g6[:, 4, META + P:T], g7[:, 0, META + P:T], start=True, stop=True)
                mm(G[3][0:n0, 2 * P:2 * P + n0], g6[:, 4, 0:n0], g7[:, 0, 0:n0], start=True,
                   stop=True).then_inc(ev("cb_done"), 1)
                dense_half(0, 0)
                pe.wait_ge(ev("xd_ready"), i * 3 + 3)
                mm(G[0], b_tok[0:n0, 0, :], xef[0:n0, 0, :], start=True, stop=True)
                mm(G[1], b_tok[:, 1, :], xef[:, 1, :], start=True, stop=True)
                mm(G[2], b_tok[:, 1, :], xeb[:, 0, :], start=True, stop=True)
                pe.wait_ge(ev("cb_ready"), after["cb_ready"] + i + 1)
                mm(G[3], b_tok[:, 2, :], xeb[:, 1, :], start=True, stop=True).then_inc(ev("st_done"), 1)
                dense_half(0, 1)
                pe.wait_ge(ev("st_ready"), i + 1)
                for q, ck in enumerate((1, 2, 0)):
                    t0, nt = TOK[ck]
                    pe.wait_ge(ev("mg_ready"), i * 3 + q + 1)
                    if q:
                        pe.wait_ge(ev("yt_read"), i * 3 + q)
                    if ck == 0:
                        carry_wait()
                    if ck:
                        for half in range(2):
                            f, b = [work2[:, x, 4 * half:4 * half + 4, :] for x in range(2)]
                            mm(G[half], m_gt, f, start=True, stop=False)
                            mm(G[half], m_lt, b, start=False, stop=True).then_inc(ev("E_done"), 1)
                    else:
                        mm(G[0][0:nt, 0:P], m_gt[0:nt, 0:nt], small2[0], start=True, stop=False)
                        mm(G[0][0:nt, 0:P], m_lt[0:nt, 0:nt], small2[1], start=False, stop=True).then_inc(ev("E_done"), 1)
                    if q < 2:
                        dense_half(1, q)
                    pe.wait_ge(ev("M_ready"), after["M_ready"] + i * 3 + q + 1)
                    if ck == 0:
                        carry_wait()
                    for h in range(8):
                        hc = slice(h * 64, (h + 1) * 64)
                        lf = work2[:, 0, h, :] if ck else small2[0][:, h, :]
                        lb = work2[:, 1, h, :] if ck else small2[1][:, h, :]
                        mm(G[2][0:nt, hc], lf, xdf[0:nt, ck, hc], start=True, stop=False)
                        ins = mm(G[2][0:nt, hc], lb, xdb[0:nt, ck, hc], start=False, stop=True)
                    if ck:
                        ins = mm(G[3], g7[:, 0, t0:t0 + nt], st[:, ck - 1, :], start=True, stop=True)
                    if ck < 2:
                        ins = mm(G[0][0:nt, :], g7[:, 0, t0:t0 + nt], st[:, 3 - ck, :], start=True, stop=True)
                    ins.then_inc(ev("y_done"), 1)
                    pe.wait_ge(ev("y_ready"), i * 3 + q + 1)
                    if ck == 0:
                        carry_wait()
                    for b in range(4):
                        ins = nc.tensor.transpose(G[1][:, b * P:b * P + nt], ytok[0:nt, ck, b * P:(b + 1) * P],
                                                  ident[0:nt, 0:nt])
                    ins.then_inc(ev("yt_done"), 1)
            with pe.Fori(0, SG - 1) as i:
                group(i)
            group(SG - 1)
            n[0] += 2 * SG
            release[:] = [("group_left", after["group_left"] + SG + 1)] * 4
            for g in range(4):
                for j in range(2):
                    k, m = n[0] % 2, n[0] // 2
                    pe.wait_ge(slot_loaded[k], 16 * (m + 1))
                    if g == 0:
                        pe.wait_ge(ev("yn_ready"), j + 1)
                    if j == 0:
                        pe.wait_ge(copied[k], m)
                        pe.wait_ge(copied[1 - k], (n[0] + 1) // 2)
                        out_pair = pair[k]
                    for b in range(2):
                        for c in range(DC):
                            ins = mm(out_pair[:, b, 0:T], slot8[k][:, c, b * P:(b + 1) * P], yT[:, 8 * j + c, :],
                                     start=j == 0 and c == 0, stop=j == 1 and c == DC - 1)
                    ins.then_inc(panel_done[k], 1)
                    n[0] += 1
                if g == 0:
                    pe.wait_ge(ev("sq_ready"), 9)
                    sum_parts(use(0, "rs_ready", 7), sqy, 16, T).then_inc(ev("sum_ready"), 1)
            pe.wait_ge(ev("merged_ready"), after["merged_ready"] + 1)
            dense_panels(4, lambda c: bs[:, c, :], T)
            pe.wait_ge(ev("sq_ready"), 10)
            sum_parts(use(1, "rs_ready", 8), sq, DC, T).then_inc(ev("sum_ready"), 1)
            pe.wait_ge(ev("hn_ready"), after["hn_ready"] + 1)
            bank = use(0, "lg_copied", 1)
            for ck, (t0, nt) in enumerate(TOK):
                for c in range(DC):
                    ins = mm(bank[0:nt, ck * E:(ck + 1) * E], uT[:, c, t0:t0 + nt], w_r[:, c, :],
                             start=c == 0, stop=c == DC - 1)
            ins.then_inc(ev("lg_done"), 1)
            for q in range(6):
                ck, half = q // 2, q % 2
                t0, nt = TOK[ck]
                bank = use(2 + half, "hn_tok_copied", q + 1)
                for b in range(4):
                    ins = nc.tensor.transpose(bank[0:nt, b * P:(b + 1) * P], uT[:, 4 * half + b, t0:t0 + nt], ident)
                ins.then_inc(ev("hn_turned"), 1)
            pe.wait_ge(ev("aff_ready"), after["aff_ready"] + 1)
            bank = use(1, "affT_copied", 1)
            for ck, (t0, nt) in enumerate(TOK):
                ins = nc.tensor.transpose(bank[0:E, t0:t0 + nt], aff[0:nt, ck, 0:E], ident[0:nt, 0:nt])
            ins.then_inc(ev("aff_turned"), 1)
            for q in range(4):
                tb, half = q // 2, q % 2
                bank = use(2 + half, "hacc_copied", q + 1)
                for b in range(4):
                    ins = nc.tensor.transpose(bank[:, b * P:(b + 1) * P],
                                              hT[:, 4 * half + b, META + tb * P:META + (tb + 1) * P], ident)
                ins.then_inc(ev("hacc_turned"), 1)
            pe.wait_ge(ev("pos_ready"), 1)
            bank = use(0, "pos_copied", 1)
            for ck, (t0, nt) in enumerate(TOK):
                ins = nc.tensor.transpose(bank[0:nt, ck * E:(ck + 1) * E], pos[0:E, t0:t0 + nt], ident[0:E, 0:E])
            ins.then_inc(ev("pos_turned"), 1)
            def gather():
                for c in range(DC):
                    for ck, (t0, nt) in enumerate(TOK):
                        ins = mm(G[0][:, c * CAP:(c + 1) * CAP], hn_tok[0:nt, ck, c * P:(c + 1) * P], oh[0:nt, ck, :],
                                 start=ck == 0, stop=ck == 2)
                ins.then_inc(ev("gathered"), 1)

            pe.wait_ge(ev("hacc_copied"), after["hacc_copied"] + 4)
            pe.wait_ge(ev("hn_tok_copied"), after["hn_tok_copied"] + 6)
            pe.wait_ge(ev("pos_copied"), 1)
            pe.wait_ge(ev("oh_ready"), after["oh_ready"] + 1)
            gather()
            with pe.Fori(0, E) as e:
                pe.wait_ge(ev("xg_ready"), after["xg_ready"] + e + 1)
                pe.wait_ge(ev("acc_done"), after["acc_done"] + e + 1)
                for p in range(4):
                    for q in (2 * p, 2 * p + 1):
                        pe.wait_ge(ring_loaded[q % RING], e * 32 + 16 * (q // RING + 1))
                    for c in range(DC):
                        for x in range(2):
                            k = (2 * p + x) % RING
                            ins = mm(psum[64 * x:64 * x + CAP, p, :], xg[:, c, :], r_up[k][:, c, :],
                                     start=c == 0, stop=c == DC - 1)
                            if c == DC - 1:
                                ins.then_inc(ring_done[k], 1)
                pe.wait_ge(ev("ohs_ready"), e + 1)
                pe.wait_ge(ev("oh_ready"), after["oh_ready"] + e + 2)
                gather()
                for tb in range(2):
                    ins = nc.tensor.transpose(G[1][0:CAP, tb * P:(tb + 1) * P], ohs[:, tb, :], ident)
                ins.then_inc(ev("oh_turned"), 1)
                for x in range(2):
                    pe.wait_ge(ev("h_ready"), after["h_ready"] + e * 4 + 2 * x + 2)
                    if x == 0:
                        bank = G[3]
                    else:
                        pe.wait_ge(ev("ot_copied"), e + 1)
                        bank = G[1]
                    for b in range(8):
                        src = h_row[0:CAP, 2 * x + b // 4, (b % 4) * P:(b % 4 + 1) * P]
                        if b == 0:
                            mm(bank[:, 0:CAP], src, ident[0:CAP, 0:CAP], start=True, stop=True)
                        else:
                            ins = nc.tensor.transpose(bank[:, b * CAP:(b + 1) * CAP], src, ident[0:CAP, 0:CAP])
                    ins.then_inc(ev("h_turned"), 1)
                for q in range(8, 12):
                    k = q % RING
                    pe.wait_ge(ring_loaded[k], e * 32 + 32)
                    if q % 2 == 0:
                        pe.wait_ge(ev("hx_copied"), e * 2 + (q - 8) // 2 + 1)
                    for c in range(4):
                        f = 4 * (q - 8) + c
                        for half in range(2):
                            ins = mm(G[2][64 * half:64 * half + CAP, :], hx[:, f, :],
                                     r_dn[k][:, c, half * 512:(half + 1) * 512], start=f == 0, stop=f == EB - 1)
                    ins.then_inc(ring_done[k], 1)
                pe.wait_ge(ev("ex_out"), after["ex_out"] + e + 1)
                for tb in range(2):
                    for half in range(2):
                        ins = mm(psum[:, 2 * tb + half, :], otT[0:CAP, tb * P:(tb + 1) * P],
                                 ysb[0:CAP, half * 512:(half + 1) * 512], start=True, stop=True)
                ins.then_inc(ev("scattered"), 1)

        @block.scalar
        def _(act):
            A = nc.scalar.activation
            n = [0]

            nc.scalar.preload_act_table_set("natural_log_exp_and_others")
            for tb in range(2):
                act.dma_start(xtok[:, tb, :], a["x"][0, tb * P:(tb + 1) * P, :]).then_inc(ev("x_loaded"), 16)
            act.dma_start(meta_tok[0:META, :], a["meta_tokens_2"]).then_inc(ev("x_loaded"), 16)
            for dst, src in par_loads():
                act.dma_start(dst, src).then_inc(ev("par_loaded"), 16)
            with nc.allow_non_contiguous_dma(reason="eight gate columns"):
                act.dma_start(w_ba, w_in_v[:, :, 3328:3336]).then_inc(ev("ba_loaded"), 16)
            for dst, src in ((bc_row[:, 0:4], a["swa_sinks"]), (bc_row[:, 4:8], a["dn_a_log"]),
                             (bc_row[:, 8:12], a["dn_dt_bias"])):
                act.dma_start(dst, src.to_broadcast([P, 4])).then_inc(ev("rows_loaded"), 16)
            with nc.allow_non_contiguous_dma(reason="small columns and rows"):
                act.dma_start(w_dt, a["w_in_2"][0].rearrange("(c p) n -> p c n", p=P)[:, :, 7168:7232]).then_inc(ev("small_loaded"), 16)
                act.dma_start(w_r, a["w_router_2"][0].rearrange("(c p) n -> p c n", p=P)).then_inc(ev("small_loaded"), 16)
                act.dma_start(row_dt, a["ssm_dt_bias_2"].rearrange("a x h -> a (x h)").to_broadcast([P, 2 * SH])).then_inc(ev("small_loaded"), 16)
                act.dma_start(row_al, a["ssm_a_log_2"].rearrange("a x h -> a (x h)").to_broadcast([P, 2 * SH])).then_inc(ev("small_loaded"), 16)
                dv = a["ssm_d_2"].rearrange("a (b x) -> a x b", x=2)
                for x in range(2):
                    act.dma_start(d_col[64 * x:64 * x + 64, :], dv[:, x, :].to_broadcast([64, 16])).then_inc(ev("d_loaded"), 16)

            def copy_panels(count, dst):
                base = n[0]

                def one(k, m, blk, i=None):
                    act.wait_ge(panel_done[k], m + 1 if i is None else i + (m + 1))
                    d = dst(blk)
                    A(d, pair[k][:, :, 0:d.shape[2]], ACT.Copy).then_inc(copied[k], 1)

                if count > 1:
                    with act.Fori(0, count // 2) as i:
                        for j in range(2):
                            one((base + j) % 2, (base + j) // 2, i * 4 + 2 * j, i)
                n[0] += 2 * (count // 2)
                if count % 2:
                    one(n[0] % 2, n[0] // 2, 2 * (count - 1))
                    n[0] += 1

            def sigmoid_ln(tmp, x, name):
                A(tmp, x, ACT.Abs)
                act.drain()
                A(tmp, tmp, ACT.Exp, scale=-1.0)
                act.drain()
                A(tmp, tmp, ACT.Ln, bias=ones[0:tmp.shape[0], 0:1]).then_inc(ev(name + "_ln"), 1)

            def sigmoid(tmp, x, name, count=1, dst=None):
                sigmoid_ln(tmp, x, name)
                act.wait_ge(ev(name + "_arg"), count)
                return A(tmp if dst is None else dst, tmp, ACT.Exp)

            def norm_scale(i, b, width, scale=1.0 / D):
                act.wait_ge(ev("sum_ready"), i)
                A(rs[:, 0:width], G[b][:, 0:width], ACT.Ln, scale=scale, bias=eps_t)
                act.drain()
                A(rs[:, 0:width], rs[:, 0:width], ACT.Exp, scale=-0.5).then_inc(ev("rs_ready"), 1)

            act.wait_ge(ev("x_copied"), 4)
            act.wait_ge(ev("eps_ready"), 1)
            A(sq[:, :, 0:S], hT[:, :, META:T], ACT.Square).then_inc(ev("sq_ready"), 1)
            norm_scale(1, 0, S)
            act.wait_ge(ev("ba_ready"), 1)
            A(gates1[:, :, 0:8], gates1[:, :, 0:8], ACT.Exp)
            A(bc_row[:, 4:8], bc_row[:, 4:8], ACT.Exp)
            act.drain()
            act.nop().then_inc(ev("gate_exp"), 1)
            act.wait_ge(ev("gate_w"), 1)
            A(gates1[:, :, 16:20], gates1[:, :, 16:20], ACT.Ln).then_inc(ev("gate_ln"), 1)
            copy_panels(7, lambda blk: raw1[:, bass.ds(blk, 2), 3:3 + S])
            act.drain()
            act.nop().then_inc(ev("raw1_ready"), 1)
            for qb in range(2):
                w = P * (qb + 1)
                act.wait_ge(ev("shifted"), qb + 1)
                A(esink, esink, ACT.Exp)
                A(sc[:, 0:NH * w], sc[:, 0:NH * w], ACT.Exp).then_inc(ev("exps_ready"), 1)
                copy_panels(2 + qb, lambda blk: raw1[:, bass.ds(blk + 14 + 4 * qb, 2), 3:3 + S])
                for g4 in range(2 * (qb + 1)):
                    act.wait_ge(ev("probsT_done"), (2 if qb else 0) + g4 + 1)
                    A(pT[:, g4 * 512:(g4 + 1) * 512], G[g4 % 4], ACT.Copy).then_inc(ev("probsT_copied"), 1)
            act.wait_ge(ev("conv_ready"), 1)
            act.wait_ge(ev("heads_copied"), 2)
            qf = qkv.rearrange("p a b -> p (a b)")
            sigmoid(ex12[:, 0:8 * S], qf[:, 0:8 * S], "silu12").then_inc(ev("ex12_ready"), 1)
            copy_panels(1, lambda blk: raw1[:, bass.ds(blk + 24, 2), 3:3 + S])
            act.wait_ge(ev("silu_ready"), 1)
            A(sq_dn, qf[:, 0:8 * S], ACT.Square).then_inc(ev("sq_ready"), 1)
            sigmoid_ln(ex12[:, 8 * S:12 * S], qf[:, 8 * S:12 * S], "silu12")
            rnf = rn.rearrange("p a b -> p (a b)")
            for b in range(4):
                act.wait_ge(ev("rn_sum"), b + 1)
                A(rnf[:, b * 512:(b + 1) * 512], G[b], ACT.Ln, bias=eps_t).then_inc(ev("rn_ln"), 1)
            act.drain()
            A(rnf, rnf, ACT.Exp, scale=-0.5).then_inc(ev("rn_ready"), 1)
            act.wait_ge(ev("silu12_arg"), 2)
            A(ex12[:, 8 * S:12 * S], ex12[:, 8 * S:12 * S], ACT.Exp).then_inc(ev("ex12_ready"), 1)
            act.wait_ge(ev("gsum_done"), 1)
            A(gates1[:, 1, 12:16], G[0][:, 0:4], ACT.Exp)
            A(gates1[:, 0, 12:16], G[0][:, 4:8], ACT.Exp).then_inc(ev("gexp_read"), 1)
            for ck in range(2):
                act.wait_ge(ev("dec_done"), ck + 1)
                A(dec[ck].rearrange("p a b -> p (a b)"), G[1 + ck], ACT.Exp).then_inc(ev("dec_read"), 1)
            act.wait_ge(ev("expG_done"), 1)
            A(expG.rearrange("p a b -> p (a b)"), G[3], ACT.Exp).then_inc(ev("expG_read"), 1)
            for i in range(4):
                dst = (ktok if i < 2 else vtok2)[:, i % 2, :, :].rearrange("p a b -> p (a b)")
                act.wait_ge(ev("tok_turned"), i + 1)
                A(dst, G[2 + i % 2], ACT.Copy).then_inc(ev("tok_copied"), 1)
            for lv in range(7):
                for ck in range(2):
                    act.wait_ge(ev("Y_done"), 2 * lv + ck + 1)
                    A(Y[ck].rearrange("p a b -> p (a b)"), G[2 * ck], ACT.Copy).then_inc(ev("Y_copied"), 1)
            for ck, dst in ((0, vn0), (1, vn1)):
                act.wait_ge(ev("u_done"), ck + 1)
                A(dst.rearrange("p a b -> p (a b)"), G[ck], ACT.Copy).then_inc(ev("u_copied"), 1)
            act.wait_ge(ev("wT_done"), 1)
            A(wT.rearrange("p a b -> p (a b)"), G[2], ACT.Copy).then_inc(ev("wT_copied"), 1)
            act.wait_ge(ev("st1_done"), 1)
            A(st1.rearrange("p a b -> p (a b)"), G[3], ACT.Copy).then_inc(ev("st1_copied"), 1)
            for ck in range(2):
                act.wait_ge(ev("o_done"), ck + 1)
                if ck == 0:
                    act.wait_ge(ev("qk_ready"), 1)
                A(oT[:, :, ck * P:(ck + 1) * P], G[ck].rearrange("p (a b) -> p a b", a=4), ACT.Copy).then_inc(ev("o_copied"), 1)
            act.drain()
            A(sq_dn[:, 0:1024], oT.rearrange("p a b -> p (a b)"), ACT.Square).then_inc(ev("sq_ready"), 1)
            act.wait_ge(ev("rhs_ready"), 1)
            ezf = ez.rearrange("p a b c -> p (a b c)")
            sigmoid(ezf.rearrange("p (a b) -> p a b", a=4), raw1[:, 22:26, 3:3 + S], "z1").then_inc(ev("ez_ready"), 1)
            for b in range(2):
                act.wait_ge(ev("ro_sum"), b + 1)
                A(ro[:, b * 512:(b + 1) * 512], G[2 + b], ACT.Ln, scale=1.0 / P, bias=eps_t).then_inc(ev("ro_ln"), 1)
            act.drain()
            A(ro, ro, ACT.Exp, scale=-0.5).then_inc(ev("ro_ready"), 1)
            act.wait_ge(ev("mixed_ready"), 1)
            copy_panels(4, lambda blk: mT[:, bass.ds(blk, 2), :])
            act.drain()
            A(sq[:, :, 0:S], mT, ACT.Square).then_inc(ev("sq_ready"), 1)
            norm_scale(2, 0, S)
            act.wait_ge(ev("res_ready"), 1)
            A(sq[:, :, 0:S], hT[:, :, META:T], ACT.Square).then_inc(ev("sq_ready"), 1)
            norm_scale(3, 1, S)
            base = n[0]
            with act.Fori(0, 11) as i:
                for j in range(2):
                    k, m = (base + j) % 2, (base + j) // 2
                    act.wait_ge(panel_done[k], i + (m + 1))
                    A(raw_ff[:, bass.ds(i * 2 + FB * j, 2), 2:2 + S], pair[k][:, :, 0:S], ACT.Copy).then_inc(copied[k], 1)
                act.wait_ge(ev("gelu_in"), i + 1)
                sigmoid(fe, fg, "gelu", i + 1).then_inc(ev("gelu_exp"), 1)
            n[0] += 22
            base = n[0]
            with act.Fori(0, 4) as i:
                for j in range(2):
                    k, m = (base + j) % 2, (base + j) // 2
                    act.wait_ge(panel_done[k], i + (m + 1))
                    if j == 0:
                        act.nop().then_inc(copied[k], 1)
                act.wait_ge(panel_done[(base + 1) % 2], i + ((base + 1) // 2 + 1))
                A(fT[:, bass.ds(i * 2, 2), :], pair[base % 2][:, :, 0:S], ACT.Copy).then_inc(copied[(base + 1) % 2], 1)
            n[0] += 8
            act.drain()
            A(sq[:, :, 0:S], fT, ACT.Square).then_inc(ev("sq_ready"), 1)
            norm_scale(4, 2, S)

            act.wait_ge(ev("h1_ready"), 1)
            A(sq, hT, ACT.Square).then_inc(ev("sq_ready"), 1)
            norm_scale(5, 0, T)
            act.wait_ge(ev("small_loaded"), 64)
            A(row_al, row_al, ACT.Exp).then_inc(ev("row_exp"), 1)
            act.wait_ge(ev("pads_ready"), after["pads_ready"] + 4)
            copy_panels(8, lambda blk: raw_cf[:, bass.ds(blk, 2), :])
            act.drain()
            sigmoid(cc, raw_cf[:, DC:2 * DC, :], "cgate").then_inc(ev("cg_ready"), 1)
            copy_panels(12, lambda blk: xraw[:, bass.ds(blk, 2), 3:3 + T])
            act.drain()
            act.nop().then_inc(ev("xbc_ready"), 1)
            act.wait_ge(ev("dt_neg"), after["dt_neg"] + 1)
            A(dte, dte, ACT.Exp).then_inc(ev("dt_exp"), 1)
            copy_panels(4, lambda blk: zT[:, bass.ds(blk, 2), :])
            act.wait_ge(ev("dt_w"), after["dt_w"] + 1)
            A(dtw, dtw, ACT.Ln).then_inc(ev("dt_ln"), 1)
            act.wait_ge(ev("centred"), after["centred"] + 1)
            A(sq, cc, ACT.Square).then_inc(ev("sq_ready"), 1)
            norm_scale(6, 1, T)
            copy_panels(4, lambda blk: zT[:, bass.ds(blk + 8, 2), :])
            act.wait_ge(ev("sums_done"), after["sums_done"] + 1)
            A(sums[:, 0:320], G[2][:, 0:320], ACT.Exp)
            A(sums[0:META, 320:448], G[2][0:META, 320:448], ACT.Exp)
            act.drain()
            act.nop().then_inc(ev("sums_read"), 2)
            act.wait_ge(ev("ln_ready"), after["ln_ready"] + 1)
            sigmoid(sq, cc, "conf").then_inc(ev("csig_ready"), 1)
            copy_panels(2, lambda blk: bcf[:, bass.ds(blk, 2), :])
            act.wait_ge(ev("conv6"), after["conv6"] + 1)
            sigmoid(six, g6, "group", 1).then_inc(ev("sig6"), 1)
            copy_panels(2, lambda blk: bcf[:, bass.ds(blk + 4, 2), :])
            base = n[0]

            def group(i, last=False):
                def copy_panel(j):
                    k, m = (base + j) % 2, (base + j) // 2
                    act.wait_ge(panel_done[k], i + (m + 1))
                    d = gts[:, 4 * i + 2 * j:4 * i + 2 * j + 2, :] if last else gts[:, bass.ds(i * 4 + 2 * j, 2), :]
                    A(d, pair[k][:, :, 0:T], ACT.Copy).then_inc(copied[k], 1)

                if last:
                    sigmoid_ln(sqy[:, 0:DC, :], zT[:, 0:DC, :], "z2")
                act.wait_ge(ev("bt_done"), after["bt_done"] + i + 1)
                A(b_tok[:, 1:3, :], G[3][:, P:3 * P].rearrange("p (a b) -> p a b", a=2), ACT.Copy)
                A(b_tok[0:META, 0, :], G[3][0:META, 0:P], ACT.Copy)
                act.drain()
                act.nop().then_inc(ev("bt_copied"), 1)
                for q, ck in enumerate((1, 2, 0)):
                    for half in range(2 if ck else 1):
                        act.wait_ge(ev("E_done"), after["E_done"] + i * 5 + 2 * q + half + 1)
                        if ck:
                            A(work2[:, 1, 4 * half:4 * half + 4, :].rearrange("p a b -> p (a b)"), G[half],
                              ACT.Exp).then_inc(ev("ex_done"), 1)
                        else:
                            A(work2[0:META, 1, 0, :], G[0][0:META, 0:P], ACT.Exp).then_inc(ev("ex_done"), 1)
                    if q < 2:
                        copy_panel(q)
                    if last and q == 0:
                        act.wait_ge(ev("z2_arg"), 1)
                        A(sqy[:, 0:DC, :], sqy[:, 0:DC, :], ACT.Exp)
                        sigmoid(sqy[:, DC:2 * DC, :], zT[:, DC:2 * DC, :], "z2", 2)
                        act.drain()
                        act.nop().then_inc(ev("zsig_ready"), 1)
                        sigmoid_ln(bs, gts[:, 0:DC, :], "gates")
                    if last and q == 1:
                        act.wait_ge(ev("gates_arg"), 1)
                        A(gts[:, 0:DC, :], bs, ACT.Exp).then_inc(ev("gsig_ready"), 1)
                        act.drain()
                        sigmoid_ln(bs, gts[:, DC:2 * DC, :], "gates")
                        act.wait_ge(ev("yz_ready"), 1)
                        A(sqy[:, 0:12, :], sqy[:, 0:12, :], ACT.Square)
                    if not last and q == 1:
                        act.wait_ge(ev("conv6"), after["conv6"] + i + 2)
                        sigmoid_ln(six, g6, "group")
                if not last:
                    act.wait_ge(ev("group_arg"), i + 2)
                    A(six, six, ACT.Exp).then_inc(ev("sig6"), 1)

            with act.Fori(0, SG - 1) as i:
                group(i)
            group(SG - 1, last=True)
            n[0] += 2 * SG
            act.wait_ge(ev("yz_ready"), 2)
            A(sqy[:, 12:16, :], sqy[:, 12:16, :], ACT.Square)
            act.drain()
            act.nop().then_inc(ev("sq_ready"), 1)
            act.wait_ge(ev("gates_arg"), 2)
            A(gts[:, DC:2 * DC, :], bs, ACT.Exp).then_inc(ev("gsig_ready"), 1)
            act.drain()
            for g in range(4):
                k0, m0 = n[0] % 2, n[0] // 2
                k1, m1 = (n[0] + 1) % 2, (n[0] + 1) // 2
                act.wait_ge(panel_done[k0], m0 + 1)
                act.nop().then_inc(copied[k0], 1)
                act.wait_ge(panel_done[k1], m1 + 1)
                A(bs[:, 2 * g:2 * g + 2, :], pair[k0][:, :, 0:T], ACT.Copy).then_inc(copied[k1], 1)
                if g == 0:
                    norm_scale(7, 0, T, 1.0 / (2 * D))
                n[0] += 2
            act.drain()
            act.nop().then_inc(ev("bs_ready"), 1)
            copy_panels(4, lambda blk: mo[:, bass.ds(blk, 2), :])
            act.drain()
            act.nop().then_inc(ev("mo_ready"), 1)
            act.dma_start(wfin, a["w_norm_final_2"].rearrange("(a n) -> a n", a=1).to_broadcast([P, D])).then_inc(ev("wfin_loaded"), 16)
            act.wait_ge(ev("h2_ready"), after["h2_ready"] + 1)
            A(sq, hT, ACT.Square).then_inc(ev("sq_ready"), 1)
            norm_scale(8, 1, T)
            act.wait_ge(ev("hn_turned"), after["hn_turned"] + 2)
            for q in range(6):
                nt = TOK[q // 2][1]
                act.wait_ge(ev("hn_turned"), after["hn_turned"] + q + 1)
                A(hn_tok[0:nt, q // 2, (q % 2) * 512:(q % 2 + 1) * 512], G[2 + q % 2][0:nt, :], ACT.Copy).then_inc(ev("hn_tok_copied"), 1)
                if q == 1:
                    act.wait_ge(ev("lg_shifted"), after["lg_shifted"] + 1)
                    A(lg, lg, ACT.Exp).then_inc(ev("lg_exp"), 1)

            def copy_gathered(v):
                act.wait_ge(ev("gathered"), after["gathered"] + v)
                A(xg.rearrange("p a b -> p (a b)"), G[0][:, 0:DC * CAP], ACT.Copy).then_inc(ev("xg_ready"), 1)

            copy_gathered(1)
            with act.Fori(0, E) as e:
                for p in range(4):
                    q = 2 * p + 1
                    act.wait_ge(ring_done[q % RING], e * 2 + q // RING + 1)
                    A(up_row[0:CAP, p % 2, :], psum[64:64 + CAP, p, :], ACT.Copy)
                    sigmoid(es[0:CAP, p % 2, :], psum[0:CAP, p, :], "expert", e * 4 + p + 1).then_inc(ev("esig_ready"), 1)
                copy_gathered(e + 2)
                act.wait_ge(ev("oh_turned"), after["oh_turned"] + e + 1)
                A(otT[0:CAP, :], G[1][0:CAP, 0:S], ACT.Copy).then_inc(ev("ot_copied"), 1)
                for x in range(2):
                    act.wait_ge(ev("h_turned"), e * 2 + x + 1)
                    A(hx[:, 8 * x:8 * x + 8, :].rearrange("p a b -> p (a b)"), G[3 - 2 * x][:, 0:8 * CAP],
                      ACT.Copy).then_inc(ev("hx_copied"), 1)
                act.wait_ge(ring_done[11 % RING], e * 2 + 2)
                for half in range(2):
                    A(ysb[0:CAP, half * 512:(half + 1) * 512], psum[64 * half:64 * half + CAP, 6, :], ACT.Copy)
                act.drain()
                act.nop().then_inc(ev("ex_out"), 1)
            act.wait_ge(ev("acc_done"), after["acc_done"] + E + 1)
            for tb in range(2):
                A(hn_tok[:, tb, :], hacc[:, tb, :], ACT.Square, accum_out=ss[:, tb:tb + 1])
            act.drain()
            A(ss[:, 0:2], ss[:, 0:2], ACT.Ln, scale=1.0 / D, bias=eps_t)
            act.drain()
            A(ss[:, 0:2], ss[:, 0:2], ACT.Exp, scale=-0.5).then_inc(ev("rfin_ready"), 1)

        @block.vector
        def _(dve):
            v = nc.vector
            TS, TT, STT, CP = v.tensor_scalar, v.tensor_tensor, v.scalar_tensor_tensor, v.tensor_copy
            MUL, ADD, SUB, MAX = ALU.mult, ALU.add, ALU.subtract, ALU.max

            def sigmoid_arg(tmp, x, name, count=1):
                dve.wait_ge(ev(name + "_ln"), count)
                STT(tmp, x, 0.0, tmp, ALU.min, SUB).then_inc(ev(name + "_arg"), 1)

            v.memset(eps_t, EPS).then_inc(ev("eps_ready"), 1)
            for q in range(2):
                dve.wait_ge(ev("par_turned"), q + 1)
                w = min(4, PAR_T - 4 * q) * P
                w = min(w, PAR_N - 4 * q * P)
                CP(par[:, q * 512:q * 512 + w], G[q][:, 0:w]).then_inc(ev("par_copied"), 1)
            for tb in range(2):
                for c4 in range(2):
                    dve.wait_ge(ev("x_turned"), 2 * tb + c4 + 1)
                    CP(hT[:, 4 * c4:4 * c4 + 4, META + tb * P:META + (tb + 1) * P],
                       G[2 + c4].rearrange("p (a b) -> p a b", a=4)).then_inc(ev("x_copied"), 1)
            dve.wait_ge(ev("x_turned"), 5)
            CP(hT[:, :, 0:META], G[2][:, 0:DC * META].rearrange("p (a b) -> p a b", a=DC)).then_inc(ev("x_copied"), 1)

            def normed(dst, src, name, width):
                for c in range(DC):
                    ins = STT(dst(c), src(c), pcol(name, c), rs[:, 0:width], MUL, MUL)
                return ins

            dve.drain()
            dve.wait_ge(ev("rs_ready"), 1)
            normed(lambda c: uT[:, c, 0:S], lambda c: hT[:, c, META:T], "mix_pre", S).then_inc(ev("u_ready"), 1)

            x4 = gates1[:, :, 20:24]
            dve.wait_ge(ev("ba_done"), 1)
            dve.wait_ge(ev("rows_loaded"), 48)
            CP(ba, G[1][:, 0:16].rearrange("p (a b) -> p a b", a=2)).then_inc(ev("ba_copied"), 1)
            dve.drain()
            TS(gates1[:, :, 0:4], ba[:, :, 0:4], -1.0, None, MUL)
            TT(x4, ba[:, :, 4:8], bc_row[:, 8:12].unsqueeze(1).to_broadcast([P, 2, 4]), ADD)
            dve.drain()
            STT(gates1[:, :, 4:8], x4, -1.0, x4, MUL, ALU.min).then_inc(ev("ba_ready"), 1)

            dve.wait_ge(ev("gate_exp"), 1)
            e4, w4, g4 = gates1[:, :, 4:8], gates1[:, :, 16:20], gates1[:, :, 8:12]
            beta = gates1[:, :, 0:4]
            TS(w4, e4, 1.0, None, ADD)
            TS(beta, beta, 1.0, None, ADD)
            dve.drain()
            v.reciprocal(beta, beta)
            TS(ba[:, :, 0:4], w4, 1.0, None, SUB)
            dve.drain()
            TS(ba[:, :, 4:8], ba[:, :, 0:4], 0.0, None, ALU.is_equal).then_inc(ev("gate_w"), 1)
            dve.drain()
            TT(ba[:, :, 0:4], ba[:, :, 0:4], ba[:, :, 4:8], ADD)
            dve.wait_ge(ev("gate_ln"), 1)
            TT(w4, w4, ba[:, :, 4:8], ADD)
            dve.drain()
            v.reciprocal(ba[:, :, 0:4], ba[:, :, 0:4])
            dve.drain()
            TT(w4, w4, ba[:, :, 0:4], MUL)
            dve.drain()
            TT(w4, w4, e4, MUL)
            dve.drain()
            STT(w4, x4, 0.0, w4, MAX, ADD)
            dve.drain()
            STT(g4, w4, -1.0, bc_row[:, 4:8].unsqueeze(1).to_broadcast([P, 2, 4]), MUL, MUL)
            dve.drain()
            dve.wait_ge(ev("masks_ready"), 1)
            for ck in range(2):
                ins = TT(mg[ck], bcast(m_le, 4, 1), bcast(gates1[:, ck, 8:12], P), MUL)
            ins.then_inc(ev("mg_ready"), 1)
            for ck in range(2):
                TT(bB[ck], bcast(ident, 4, 1), bcast(gates1[:, ck, 0:4], P), MUL).then_inc(ev("bd_ready"), 1)

            def delta_conv(i):
                for j in range(2):
                    dve.wait_ge(copied[(5 + j) % 2], i + ((5 + j) // 2 + 1))
                for tap in range(4):
                    for b in range(4 * i, 4 * i + 4):
                        src = raw1[:, 10 + b, tap:tap + S]
                        if tap == 0:
                            TS(qkv[:, b, :], src, pcol("dn_conv", b), None, MUL)
                        else:
                            STT(qkv[:, b, :], src, pcol("dn_conv", 12 * tap + b), qkv[:, b, :], MUL, ADD)
                    dve.drain()

            dve.wait_ge(ev("raw1_ready"), 1)
            for h in range(4):
                ins = CP(q_arr[HD * (h // 2):HD * (h // 2) + HD, h % 2, :],
                         raw1[HD * (h % 2):HD * (h % 2) + HD, h // 2, 3:3 + S])
            ins.then_inc(ev("q_ready"), 1)
            for tb in range(2):
                dve.wait_ge(ev("v_turned"), tb + 1)
                CP(vtok[:, tb, :, :], G[tb][:, 0:384].rearrange("p (a b) -> p a b", a=3)).then_inc(ev("vtok_ready"), 1)

            dve.wait_ge(ev("raw1_pad"), 1)
            dve.wait_ge(ev("bias_ready"), 1)
            allG = psum[:, 4:8, :].rearrange("p a (b c) -> p (a b) c", b=2)
            for qb in range(2):
                w = P * (qb + 1)
                s3 = sc[:, 0:NH * w].rearrange("p (a b) -> p a b", a=NH)
                dve.wait_ge(ev("scores_done"), qb + 1)
                for b in range(4):
                    STT(s3[:, 2 * b:2 * b + 2, :], allG[:, 2 * b:2 * b + 2, 0:w], HD ** -0.5,
                        bias[:, 2 * b:2 * b + 2, S - w:S], MUL, ADD)
                dve.drain()
                dve.nop().then_inc(ev("scores_read"), 1)
                v.tensor_reduce(mx, s3, AX, MAX)
                dve.drain()
                TT(mx[:, 0:4], mx[:, 0:4], bc_row[:, 0:4], MAX)
                dve.drain()
                TT(esink, bc_row[:, 0:4], mx[:, 0:4], SUB)
                TT(s3, s3, bcast(mx, w), SUB).then_inc(ev("shifted"), 1)
                dve.wait_ge(ev("exps_ready"), qb + 1)
                v.tensor_reduce(den, s3, AX, ADD)
                dve.drain()
                TT(den[:, 0:4], den[:, 0:4], esink, ADD)
                dve.drain()
                v.reciprocal(den, den)
                dve.drain()
                TT(s3, s3, bcast(den, w), MUL).then_inc(ev("probs_ready"), 1)
                delta_conv(2 * qb)
                dve.wait_ge(ev("heads_done"), qb + 1)
                CP(mixed[:, 0:4, qb * P:(qb + 1) * P], G[0].rearrange("p (a b) -> p a b", a=4)).then_inc(ev("heads_copied"), 1)
                if qb == 0:
                    delta_conv(1)
            dve.nop().then_inc(ev("conv_ready"), 1)

            qf = qkv.rearrange("p a b -> p (a b)")
            sigmoid_arg(ex12[:, 0:8 * S], qf[:, 0:8 * S], "silu12")
            dve.wait_ge(ev("ex12_ready"), 1)
            TT(qf[:, 0:8 * S], ex12[:, 0:8 * S], qf[:, 0:8 * S], MUL).then_inc(ev("silu_ready"), 1)
            sigmoid_arg(ex12[:, 8 * S:12 * S], qf[:, 8 * S:12 * S], "silu12", 2)
            dve.wait_ge(ev("rn_ready"), 1)
            rnf = rn.rearrange("p a b -> p (a b)")
            dve.drain()
            STT(qf[:, 0:4 * S], qf[:, 0:4 * S], float(P) ** -0.5, rnf[:, 0:4 * S], MUL, MUL)
            TT(qf[:, 4 * S:8 * S], qf[:, 4 * S:8 * S], rnf[:, 4 * S:8 * S], MUL).then_inc(ev("qk_ready"), 1)
            dve.wait_ge(ev("ex12_ready"), 2)
            TT(qf[:, 8 * S:12 * S], ex12[:, 8 * S:12 * S], qf[:, 8 * S:12 * S], MUL).then_inc(ev("silu_ready"), 1)
            dve.drain()
            for ck in range(2):
                CP(X[ck], bcast(ident, 4, 1))
                CP(XT[ck], bcast(ident, 4, 1))
            for ck in range(2):
                dve.wait_ge(ev("dec_read"), ck + 1)
                TT(dec[ck], dec[ck], bcast(m_le, 4, 1), MUL)
            for ck in range(2):
                dve.wait_ge(ev("bB_done"), ck + 1)
                TT(bB[ck], qkv[:, 4:8, ck * P:(ck + 1) * P], G[ck].rearrange("p (a b) -> p a b", a=4),
                   MUL).then_inc(ev("kb_ready"), 1)
            dve.wait_ge(ev("levels_ready"), 1)
            for ck in range(2):
                dve.wait_ge(ev("kk_done"), ck + 1)
                TT(LT[ck], dec[ck], G[0].rearrange("p (a b) -> p a b", a=4), MUL).then_inc(ev("LT_ready"), 1)
                dve.wait_ge(ev("kq_done"), ck + 1)
                TT(aT[ck], dec[ck], G[1].rearrange("p (a b) -> p a b", a=4), MUL).then_inc(ev("aT_ready"), 1)
            dve.drain()
            for ck in range(2):
                TT(BT[ck], LT[ck], bcast(lvl[:, 0, :], 4, 1), MUL).then_inc(ev("BT_ready"), 1)
            dve.wait_ge(ev("gexp_read"), 1)
            TT(gates1[:, 1, 12:16], gates1[:, 1, 12:16], gates1[:, 1, 0:4], MUL)
            dve.wait_ge(ev("tok_copied"), 4)
            for ck in range(2):
                TT(vb[ck], vtok2[:, ck, :, :], bcast(gates1[:, ck, 0:4], P), MUL)
            dve.drain()
            TT(kbg, ktok[:, 1, :, :], bcast(gates1[:, 1, 12:16], P), MUL)
            TT(kdec, ktok[:, 0, :, :], bcast(gates1[:, 0, 12:16], P), MUL)
            dve.wait_ge(ev("expG_read"), 1)
            TT(qdec, qkv[:, 0:4, P:2 * P], expG, MUL)
            dve.drain()
            dve.nop().then_inc(ev("rhs_ready"), 1)
            for lv in range(7):
                for ck in range(2):
                    g3 = lambda b: G[b].rearrange("p (a b) -> p a b", a=4)
                    dve.wait_ge(ev("PT_done"), 2 * lv + ck + 1)
                    if lv < 6:
                        dve.wait_ge(ev("PX_done"), 2 * lv + ck + 1)
                        TT(X[ck], X[ck], g3(2 * ck), SUB).then_inc(ev("X_ready"), 1)
                        TT(BT[ck], LT[ck], bcast(lvl[:, lv + 1, :], 4, 1), MUL).then_inc(ev("BT_ready"), 1)
                    TT(XT[ck], XT[ck], g3(2 * ck + 1), SUB).then_inc(ev("XT_ready"), 1)
                dve.drain()
            dve.wait_ge(ev("u_copied"), 2)
            dve.wait_ge(ev("ws_done"), 1)
            TT(vn1, vn1, G[2].rearrange("p (a b) -> p a b", a=4), SUB).then_inc(ev("vn1_ready"), 1)
            sigmoid_arg(ez.rearrange("p a b c -> p (a b c)").rearrange("p (a b) -> p a b", a=4), raw1[:, 22:26, 3:3 + S], "z1")
            dve.wait_ge(ev("ez_ready"), 1)
            TT(sz, ez.rearrange("p a b c -> p (a b c)").rearrange("p (a b) -> p a b", a=4),
               raw1[:, 22:26, 3:3 + S], MUL)
            dve.wait_ge(ev("ro_ready"), 1)
            STT(oT, oT, pcol("dn_norm"), ro.rearrange("p (a b) -> p a b", a=4), MUL, MUL)
            dve.drain()
            TT(mixed[:, 4:8, :], oT, sz, MUL).then_inc(ev("mixed_ready"), 1)

            def residual(src, name, lo, width):
                normed(lambda c: src[:, c, 0:width], lambda c: src[:, c, 0:width], name, width)
                dve.drain()
                return TT(hT[:, :, lo:lo + width], hT[:, :, lo:lo + width], src[:, :, 0:width], ADD)

            dve.wait_ge(ev("rs_ready"), 2)
            residual(mT, "mix_post", META, S).then_inc(ev("res_ready"), 1)
            dve.wait_ge(ev("rs_ready"), 3)
            dve.drain()
            normed(lambda c: uT[:, c, 0:S], lambda c: hT[:, c, META:T], "ffn_pre", S).then_inc(ev("u_ready"), 1)
            dve.wait_ge(ev("ffn_pad"), 1)
            base = 13 + 4
            with dve.Fori(0, 11) as i:
                for j in range(2):
                    dve.wait_ge(copied[(base + j) % 2], i + ((base + j) // 2 + 1))
                for tap in range(3):
                    for half, dst in enumerate((gx, ux)):
                        for b in range(2):
                            off = FB * half + b
                            src = raw_ff[:, bass.ds(i * 2 + off, 1), tap:tap + S]
                            d = dst[:, b:b + 1, :]
                            w = pdyn("ffn_conv", i * 2 + (2 * FB * tap + off))
                            if tap == 0:
                                TS(d, src, w, pdyn("ffn_b", i * 2 + off), MUL, ADD)
                            else:
                                STT(d, src, w, d, MUL, ADD)
                    dve.drain()
                TT(fg, gx, gx, MUL)
                dve.drain()
                TS(fg, fg, GELU_A * GELU_B, GELU_B, MUL, ADD)
                dve.drain()
                TT(fg, fg, gx, MUL).then_inc(ev("gelu_in"), 1)
                sigmoid_arg(fe, fg, "gelu", i + 1)
                dve.wait_ge(ev("gelu_exp"), i + 1)
                TT(gx, fe, gx, MUL)
                dve.drain()
                TT(hid[:, bass.ds(i * 2, 2), :], gx, ux, MUL).then_inc(ev("hid_ready"), 1)
                dve.drain()
            dve.wait_ge(ev("rs_ready"), 4)
            residual(fT, "ffn_post", META, S).then_inc(ev("h1_ready"), 1)

            dve.wait_ge(ev("rs_ready"), 5)
            dve.drain()
            normed(lambda c: uT[:, c, :], lambda c: hT[:, c, :], "mix2", T).then_inc(ev("u_ready"), 1)
            dve.wait_ge(ev("small_loaded"), 64)
            dve.wait_ge(ev("row_exp"), after["row_exp"] + 1)
            v.memset(dtx, 0.0)
            dve.drain()
            dve.wait_ge(ev("dt_done"), after["dt_done"] + 1)
            for ck, (t0, nt) in enumerate(TOK):
                ins = TT(dtx[0:nt, ck, :], G[1][0:nt, ck * 64:(ck + 1) * 64], row_dt[0:nt, :], ADD)
            ins.then_inc(ev("dt_copied"), 1)
            dve.drain()
            STT(dte, dtx, -1.0, dtx, MUL, ALU.min).then_inc(ev("dt_neg"), 1)
            dve.wait_ge(ev("pads_ready"), after["pads_ready"] + 4)
            sigmoid_arg(cc, raw_cf[:, DC:2 * DC, :], "cgate")
            dve.wait_ge(ev("cg_ready"), after["cg_ready"] + 1)
            TT(cpad[:, :, 15:15 + T], raw_cf[:, 0:DC, :], cc, MUL)
            dve.drain()
            for c in range(DC):
                TS(cc[:, c, :], cpad[:, c, 0:T], pcol("conf_w", c), pcol("conf_b", c), MUL, ADD)
            with dve.Fori(1, 31) as k:
                dve.drain()
                for c in range(DC):
                    STT(cc[:, c, :], cpad[:, c, bass.ds(k, T)], pdyn("conf_w", k * DC + c), cc[:, c, :], MUL, ADD)
            dve.drain()
            dve.nop().then_inc(ev("conf_conv"), 1)
            dve.wait_ge(ev("dt_exp"), after["dt_exp"] + 1)
            TS(dtw, dte, 1.0, None, ADD)
            dve.drain()
            TS(dta, dtw, 1.0, None, SUB)
            dve.drain()
            TS(dts, dta, 0.0, None, ALU.is_equal).then_inc(ev("dt_w"), 1)
            dve.drain()
            TT(dta, dta, dts, ADD)
            dve.drain()
            v.reciprocal(dta, dta)
            dve.wait_ge(ev("dt_ln"), after["dt_ln"] + 1)
            TT(dtw, dtw, dts, ADD)
            dve.drain()
            TT(dtw, dtw, dta, MUL)
            dve.drain()
            TT(dtw, dtw, dte, MUL)
            dve.drain()
            STT(dts, dtx, 0.0, dtw, MAX, ADD)
            dve.drain()
            STT(dta, dts, -1.0, row_al.unsqueeze(1).to_broadcast([P, 3, 64]), MUL, MUL).then_inc(ev("dta_ready"), 1)
            dve.wait_ge(ev("mean_done"), after["mean_done"] + 1)
            TS(rs[:, 0:T], G[0][:, 0:T], 1.0 / D, None, MUL).then_inc(ev("mean_read"), 1)
            dve.drain()
            TT(cc, cc, rs[:, 0:T].unsqueeze(1).to_broadcast([P, DC, T]), SUB).then_inc(ev("centred"), 1)
            dve.wait_ge(ev("rs_ready"), 6)
            dve.drain()
            normed(lambda c: cc[:, c, :], lambda c: cc[:, c, :], "ln_g", T)
            dve.drain()
            for c in range(DC):
                ins = TS(cc[:, c, :], cc[:, c, :], pcol("ln_b", c), None, ADD)
            ins.then_inc(ev("ln_ready"), 1)
            dve.drain()
            sigmoid_arg(sq, cc, "conf")
            dve.wait_ge(ev("csig_ready"), after["csig_ready"] + 1)
            TT(cc, cc, sq, MUL).then_inc(ev("conf_ready"), 1)
            dve.wait_ge(ev("sums_read"), after["sums_read"] + 2)
            dve.drain()
            TT(sums[:, 64:128], sums[:, 64:128], dts[:, 1, :], MUL)
            TT(sums[:, 256:320], sums[:, 256:320], dts[:, 2, :], MUL)
            TT(sums[0:META, 384:448], sums[0:META, 384:448], dts[0:META, 0, :], MUL)

            def conv6(i, taps):
                blocks = [i * 4, i * 4 + 1, i * 4 + 2, i * 4 + 3, i + 16, i + 20]
                for tap in taps:
                    for b, blk in enumerate(blocks):
                        src = xraw[:, bass.ds(blk, 1), tap:tap + T]
                        w = pdyn("ssm_w", blk + 24 * tap)
                        if tap == 0:
                            TS(g6[:, b:b + 1, :], src, w, pdyn("ssm_b", blk), MUL, ADD)
                        else:
                            STT(g6[:, b:b + 1, :], src, w, g6[:, b:b + 1, :], MUL, ADD)
                    dve.drain()

            dve.wait_ge(ev("xbc_ready"), after["xbc_ready"] + 1)
            dve.wait_ge(ev("d_loaded"), 32)
            dve.drain()
            conv6(0, range(7))
            dve.nop().then_inc(ev("conv6"), 1)
            sigmoid_arg(six, g6, "group", 1)
            dve.wait_ge(panel_done[1], GROUP_PANEL // 2)
            dve.wait_ge(panel_done[0], (GROUP_PANEL + 1) // 2)
            dve.nop().then_inc(ev("group_left"), 1)

            def gated(lo, hi):
                dve.drain()
                TT(sqy[:, lo:hi, :], yT[:, lo:hi, :], zT[:, lo:hi, :], MUL).then_inc(ev("yz_ready"), 1)
                for c in range(lo, hi):
                    if c == lo:
                        dve.drain()
                    ins = STT(yT[:, c, :], yT[:, c, :], pcol("ssm_norm", c), zT[:, c, :], MUL, MUL)
                ins.then_inc(ev("yn_ready"), 1)

            def group(i, last=False):
                dve.wait_ge(ev("sig6"), after["sig6"] + i + 1)
                TT(g7[:, 0, :], g6[:, 5, :], six[:, 5, :], MUL)
                TT(g6[:, 0:5, :], g6[:, 0:5, :], six[:, 0:5, :], MUL)
                dve.drain()
                dve.nop().then_inc(ev("g6_ready"), 1)
                for b in range(4):
                    TS(yT[:, bass.ds(i * 4 + b, 1), :], g6[:, b:b + 1, :], d_col[:, bass.ds(i * 4 + b, 1)], None, MUL)
                for ck, (t0, nt) in enumerate(TOK):
                    dve.wait_ge(ev("xt_done"), after["xt_done"] + i * 3 + ck + 1)
                    src = G[ck][0:nt, :].rearrange("p (h c) -> p h c", h=8)

                    def scaled(dst, tile, off):
                        wt = tile[0:nt, bass.ds(i * 8 + off, 8)]
                        return TT(dst.rearrange("p (h c) -> p h c", h=8), src,
                                  wt.unsqueeze(2).to_broadcast([nt, 8, 64]), MUL)

                    dflat = dts.rearrange("p a b -> p (a b)")
                    so = (384, 64, 256)[ck]
                    if ck < 2:
                        scaled(xef[0:nt, ck, :], sums, so)
                    if ck > 0:
                        scaled(xeb[0:nt, ck - 1, :], sums, so + 32)
                    scaled(xdb[0:nt, ck, :], dflat, ck * 64 + 32)
                    scaled(xdf[0:nt, ck, :], dflat, ck * 64).then_inc(ev("xd_ready"), 1)
                dve.wait_ge(ev("cb_done"), after["cb_done"] + i + 1)
                for dst, mask in ((cbf, m_le), (cbb, m_ge)):
                    TT(dst[:, 0:2 * P].rearrange("p (a b) -> p a b", a=2),
                       G[3][:, 0:2 * P].rearrange("p (a b) -> p a b", a=2), bcast(mask, 2, 1), MUL)
                    ins = TT(dst[0:META, 2 * P:2 * P + META], G[3][0:META, 2 * P:2 * P + META], mask[0:META, 0:META], MUL)
                ins.then_inc(ev("cb_ready"), 1)

                def decay_inputs(ck):
                    nt = TOK[ck][1]
                    for x, mask in ((0, m_le), (1, m_ge)):
                        at = dta[0:nt, ck, bass.ds(i * 8 + 32 * x, 8)]
                        dst = work2[:, x, :, :] if ck else small2[x]
                        ins = TT(dst, mask[0:nt, 0:nt].unsqueeze(1).to_broadcast([nt, 8, nt]),
                                 at.unsqueeze(2).to_broadcast([nt, 8, nt]), MUL)
                    ins.then_inc(ev("mg_ready"), 1)

                decay_inputs(1)
                dve.wait_ge(ev("st_done"), after["st_done"] + i + 1)
                CP(st[:, 0, :], G[0])
                CP(st[:, 2, :], G[3])
                dve.drain()
                for x, (b, off) in enumerate(((1, 128), (2, 160))):
                    wt = sums[:, bass.ds(i * 8 + off, 8)].unsqueeze(2).to_broadcast([P, 8, 64])
                    TT(st[:, 1 + 2 * x, :].rearrange("p (h c) -> p h c", h=8),
                       st[:, 2 * x, :].rearrange("p (h c) -> p h c", h=8), wt, MUL)
                dve.drain()
                TT(st[:, 1, :], st[:, 1, :], G[1], ADD)
                TT(st[:, 3, :], st[:, 3, :], G[2], ADD)
                dve.drain()
                dve.nop().then_inc(ev("st_ready"), 1)
                if not last:
                    conv6(i + 1, range(1))
                for q, ck in enumerate((1, 2, 0)):
                    t0, nt = TOK[ck]
                    for half in range(2 if ck else 1):
                        dve.wait_ge(ev("ex_done"), after["ex_done"] + i * 5 + 2 * q + half + 1)
                        hs = slice(4 * half, 4 * half + 4) if ck else slice(0, 8)
                        co = (2 * P, 0, P)[ck]
                        for x, cb in ((0, cbf), (1, cbb)):
                            e3 = work2[:, 1, hs, :] if ck else small2[1]
                            dst = work2[:, x, hs, :] if ck else small2[x]
                            ins = TT(dst, e3, cb[0:nt, co:co + nt].unsqueeze(1).to_broadcast([nt, hs.stop - hs.start, nt]), MUL)
                            if x == 0:
                                dve.drain()
                    ins.then_inc(ev("M_ready"), 1)
                    if not last and q == 2:
                        sigmoid_arg(six, g6, "group", i + 2)
                    if not last and q < 2:
                        conv6(i + 1, (range(1, 4), range(5, 7))[q])
                        if q == 1:
                            dve.nop().then_inc(ev("conv6"), 1)
                    if last and q == 0:
                        sigmoid_arg(sqy[:, 0:DC, :], zT[:, 0:DC, :], "z2", 1)
                        sigmoid_arg(sqy[:, DC:2 * DC, :], zT[:, DC:2 * DC, :], "z2", 2)
                    if last and q == 1:
                        sigmoid_arg(bs, gts[:, 0:DC, :], "gates", 1)
                        dve.wait_ge(ev("zsig_ready"), after["zsig_ready"] + 1)
                        TT(zT, zT, sqy, MUL)
                        gated(0, 12)
                    dve.wait_ge(ev("y_done"), after["y_done"] + i * 3 + q + 1)
                    eo = (320, 0, 192)[ck]
                    h3 = lambda ap: ap.rearrange("p (h c) -> p h c", h=8)
                    wt = lambda off: sums[0:nt, bass.ds(i * 8 + off, 8)].unsqueeze(2).to_broadcast([nt, 8, 64])
                    y = ytok[0:nt, ck, :]
                    if ck:
                        TT(h3(y), h3(G[3]), wt(eo), MUL)
                    if ck < 2:
                        TT(h3(y) if ck == 0 else h3(xef[:, 0, :]), h3(G[0][0:nt, :]), wt(eo + 32), MUL)
                    dve.drain()
                    if ck == 1:
                        TT(y, y, xef[:, 0, :], ADD)
                        dve.drain()
                    TT(y, y, G[2][0:nt, :], ADD).then_inc(ev("y_ready"), 1)
                    if q < 2:
                        decay_inputs((1, 2, 0)[q + 1])
                    dve.wait_ge(ev("yt_done"), after["yt_done"] + i * 3 + q + 1)
                    yd = yT[:, bass.ds(i * 4, 4), t0:t0 + nt]
                    TT(yd, yd, G[1].rearrange("p (a b) -> p a b", a=4)[:, :, 0:nt], ADD).then_inc(ev("yt_read"), 1)
                    if not last and q == 0:
                        dve.drain()
                        conv6(i + 1, range(4, 5))
                if last:
                    gated(12, 16)
                dve.drain()
                dve.nop().then_inc(ev("group_left"), 1)

            with dve.Fori(0, SG - 1) as i:
                group(i)
            group(SG - 1, last=True)
            sigmoid_arg(bs, gts[:, DC:2 * DC, :], "gates", 2)
            dve.wait_ge(ev("gsig_ready"), after["gsig_ready"] + 1)
            TT(bcf, bcf, gts[:, 0:DC, :], MUL)
            dve.wait_ge(ev("gsig_ready"), after["gsig_ready"] + 2)
            dve.wait_ge(ev("rs_ready"), 7)
            TT(gts[:, DC:2 * DC, :], gts[:, DC:2 * DC, :], rs[:, 0:T].unsqueeze(1).to_broadcast([P, DC, T]), MUL)
            dve.drain()
            dve.wait_ge(ev("bs_ready"), after["bs_ready"] + 1)
            TT(bs, bs, gts[:, DC:2 * DC, :], MUL)
            dve.drain()
            TT(bs, bs, bcf, ADD).then_inc(ev("merged_ready"), 1)
            dve.wait_ge(ev("mo_ready"), after["mo_ready"] + 1)
            TT(hT, hT, mo, ADD).then_inc(ev("h2_ready"), 1)
            dve.wait_ge(ev("rs_ready"), 8)
            dve.drain()
            normed(lambda c: uT[:, c, :], lambda c: hT[:, c, :], "ffn2", T).then_inc(ev("hn_ready"), 1)
            v.memset(lg, 0.0)
            v.memset(pos_t, 0.0)
            v.memset(aff, 0.0)
            dve.drain()
            dve.wait_ge(ev("lg_done"), after["lg_done"] + 1)
            for ck, (t0, nt) in enumerate(TOK):
                ins = CP(lg[0:nt, ck, :], G[0][0:nt, ck * E:(ck + 1) * E])
            ins.then_inc(ev("lg_copied"), 1)
            dve.drain()
            v.tensor_reduce(lmx, lg, AX, MAX)
            dve.drain()
            TT(lg, lg, bcast(lmx, E), SUB).then_inc(ev("lg_shifted"), 1)
            dve.wait_ge(ev("lg_exp"), after["lg_exp"] + 1)
            v.tensor_reduce(lmx, lg, AX, ADD)
            dve.drain()
            v.reciprocal(lmx, lmx)
            dve.drain()
            TT(aff[:, :, 0:E], lg, bcast(lmx, E), MUL).then_inc(ev("aff_ready"), 1)
            for q in range(4):
                dve.wait_ge(ev("hacc_turned"), after["hacc_turned"] + q + 1)
                CP(hacc[:, q // 2, (q % 2) * 512:(q % 2 + 1) * 512], G[2 + q % 2]).then_inc(ev("hacc_copied"), 1)
            dve.wait_ge(ev("aff_turned"), after["aff_turned"] + 1)
            CP(affT[0:E, :], G[1][0:E, 0:T])
            CP(left[0:E, :], G[1][0:E, 0:T]).then_inc(ev("affT_copied"), 1)
            dve.drain()
            taken = 0
            while taken < CAP:
                v.max(m8[0:E, :], left[0:E, :])
                dve.drain()
                if CAP - taken < 8:
                    v.memset(m8[0:E, CAP - taken:8], -1.0)
                    dve.drain()
                v.match_replace(left[0:E, :], m8[0:E, :], left[0:E, :], -1.0)
                dve.drain()
                taken += 8
            TT(left[0:E, :], left[0:E, :], affT[0:E, :], ALU.not_equal)
            dve.drain()
            v.memset(affT[0:E, :], 1.0)
            dve.drain()
            v.tensor_tensor_scan(pos[0:E, :], affT[0:E, :], left[0:E, :], 0.0, MUL, ADD)
            dve.drain()
            TT(pos[0:E, :], pos[0:E, :], left[0:E, :], MUL).then_inc(ev("pos_ready"), 1)
            dve.wait_ge(ev("pos_turned"), after["pos_turned"] + 1)
            for ck, (t0, nt) in enumerate(TOK):
                ins = CP(pos_t[0:nt, ck, 0:E], G[0][0:nt, ck * E:(ck + 1) * E])
            ins.then_inc(ev("pos_copied"), 1)
            dve.drain()
            dve.wait_ge(ev("iota_ready"), 1)
            dve.nop().then_inc(ev("acc_done"), 1)

            def one_hot(e):
                for ck in range(3):
                    ins = TS(oh[:, ck, :], slots_iota, pos_t[:, ck, bass.ds(e, 1)],
                             None, ALU.is_equal)
                ins.then_inc(ev("oh_ready"), 1)

            one_hot(0)
            with dve.Fori(0, E) as e:
                dve.wait_ge(ev("gathered"), after["gathered"] + e + 1)
                for tb in range(2):
                    ins = TS(ohs[:, tb, :], slots_iota, pos_t[:, 1 + tb, bass.ds(e, 1)], aff[:, 1 + tb, bass.ds(e, 1)],
                             ALU.is_equal, MUL)
                ins.then_inc(ev("ohs_ready"), 1)
                one_hot(e + 1)
                for p in range(4):
                    sigmoid_arg(es[0:CAP, p % 2, :], psum[0:CAP, p, :], "expert", e * 4 + p + 1)
                    dve.wait_ge(ev("esig_ready"), after["esig_ready"] + e * 4 + p + 1)
                    TT(es[0:CAP, p % 2, :], es[0:CAP, p % 2, :], psum[0:CAP, p, :], MUL)
                    dve.drain()
                    TT(h_row[0:CAP, p, :], es[0:CAP, p % 2, :], up_row[0:CAP, p % 2, :], MUL).then_inc(ev("h_ready"), 1)
                dve.wait_ge(ev("scattered"), after["scattered"] + e + 1)
                TT(hacc.rearrange("p a b -> p (a b)"), hacc.rearrange("p a b -> p (a b)"),
                   psum[:, 0:4, :].rearrange("p a b -> p (a b)"), ADD).then_inc(ev("acc_done"), 1)
            dve.wait_ge(ev("rfin_ready"), after["rfin_ready"] + 1)
            dve.wait_ge(ev("wfin_loaded"), 16)
            for tb in range(2):
                ins = STT(hacc[:, tb, :], hacc[:, tb, :], ss[:, tb:tb + 1], wfin, MUL, MUL)
            dve.drain()
            dve.nop().then_inc(ev("out_ready"), 1)


_OUTS = [((1, S, D), "float32")]


def kernel(**inputs):
    import numpy as np
    import concourse.bacc as bacc
    from concourse.bass_utils import run_bass_kernel_spmd

    nc = bacc.Bacc("TRN2", target_bir_lowering=False, num_devices=1)
    arrays, aps = {}, {}
    for name, value in inputs.items():
        v = np.ascontiguousarray(value)
        arrays[f"in_{name}"] = v
        aps[name] = nc.dram_tensor(f"in_{name}", v.shape, mybir.dt.from_np(v.dtype), kind="ExternalInput").ap()
    out = nc.dram_tensor("out_0", _OUTS[0][0], F32, kind="ExternalOutput").ap()
    two_blocks(nc, aps, out)
    r = run_bass_kernel_spmd(nc, [arrays], core_ids=[0])
    return r.results[0]["out_0"]
```
